# Optimizing a Trainium2 kernel written in Bass

```python
import math
import jax, jax.numpy as jnp
from jax import lax
import numpy as np

D_MODEL = 1024
BATCH = 1
SEQ = 256
DEPTH = 2

N_MIXERS = 2
N_HEADS = 16
HEAD_DIM = D_MODEL // N_HEADS
D_ATTN = N_HEADS * HEAD_DIM
DILATED_GROUPS = ((128, 1), (512, 4), (2048, 16))
N_GROUPS = len(DILATED_GROUPS)
BLOCK = 128
D_FF = 7 * D_MODEL // 2
N_EXPERTS = 8
TOP_K = 2
RMS_EPS = 1e-6

kernel_name = 'hybrid_dilated_stickbreaking_moe'

def rmsnorm(x, g):
    xf = x.astype(jnp.float32)
    y = xf * lax.rsqrt(jnp.mean(xf * xf, axis=-1, keepdims=True) + RMS_EPS)
    return (y * g.astype(jnp.float32)).astype(x.dtype)

def alibi_slopes(n):
    return jnp.asarray(2.0 ** (-8.0 * np.arange(1, n + 1) / n), dtype=jnp.float32)

def dilated_window_branch(q, k, v, window, dilation, slopes):
    b, s, h, dh = q.shape
    span = window // dilation
    n_prev = -(-span // BLOCK)
    sub_len = s // dilation
    nb = -(-sub_len // BLOCK)
    sub_pad = nb * BLOCK

    def to_sub(t):
        t = t.reshape(b, sub_len, dilation, h, dh).transpose(0, 2, 1, 3, 4)
        t = jnp.pad(t, ((0, 0), (0, 0), (0, sub_pad - sub_len), (0, 0), (0, 0)))
        return t.reshape(b, dilation, nb, BLOCK, h, dh)

    def band(t):
        tp = jnp.pad(t, ((0, 0), (0, 0), (n_prev, 0), (0, 0), (0, 0), (0, 0)))
        return jnp.concatenate([tp[:, :, i:i + nb] for i in range(n_prev + 1)], axis=3)

    qb = to_sub(q)
    kband = band(to_sub(k))
    vband = band(to_sub(v)).astype(jnp.float32)
    nk = (n_prev + 1) * BLOCK

    a = jnp.arange(BLOCK)[:, None]
    m = jnp.arange(nk)[None, :]
    rel = n_prev * BLOCK + a - m
    kpos = (jnp.arange(nb) * BLOCK)[:, None, None] + (a - rel)[None]
    valid = ((rel >= 0) & (rel <= span))[None] & (kpos >= 0)
    bias = -slopes[:, None, None] * (rel * dilation).astype(jnp.float32)[None]

    scores = jnp.einsum('brnqhd,brnkhd->brnhqk', qb, kband,
                        preferred_element_type=jnp.float32) * (1.0 / math.sqrt(dh))
    scores = jnp.where(valid[None, None, :, None], scores + bias, -jnp.inf)
    s_max = jnp.max(scores, axis=-1, keepdims=True)
    p = jnp.exp(scores - s_max)
    z = jnp.sum(p, axis=-1)
    out = jnp.einsum('brnhqk,brnkhd->brnqhd', p, vband)
    z_q = z.transpose(0, 1, 2, 4, 3)
    out = out / z_q[..., None]
    lse = s_max[..., 0].transpose(0, 1, 2, 4, 3) + jnp.log(z_q)

    out = out.reshape(b, dilation, sub_pad, h, dh)[:, :, :sub_len]
    out = out.transpose(0, 2, 1, 3, 4).reshape(b, s, h, dh)
    lse = lse.reshape(b, dilation, sub_pad, h)[:, :, :sub_len]
    lse = lse.transpose(0, 2, 1, 3).reshape(b, s, h)
    return out, lse

def dilated_mixer(hn, w_in, w_out, slopes):
    b, s, _ = hn.shape
    proj = (hn @ w_in).reshape(b, s, N_GROUPS, 3, N_HEADS, HEAD_DIM)
    outs, lses = [], []
    for g, (window, dilation) in enumerate(DILATED_GROUPS):
        o, l = dilated_window_branch(proj[:, :, g, 0], proj[:, :, g, 1], proj[:, :, g, 2],
                                     window, dilation, slopes)
        outs.append(o)
        lses.append(l)
    wts = jax.nn.softmax(jnp.stack(lses, axis=0), axis=0)
    y = jnp.sum(wts[..., None] * jnp.stack(outs, axis=0), axis=0)
    return y.reshape(b, s, D_ATTN).astype(hn.dtype) @ w_out

def stick_breaking_mixer(hn, w_qkv, w_out):
    b, s, _ = hn.shape
    qkv = (hn @ w_qkv).reshape(b, s, 3, N_HEADS, HEAD_DIM)
    q, k, v = qkv[:, :, 0], qkv[:, :, 1], qkv[:, :, 2]
    scale = 1.0 / math.sqrt(HEAD_DIM)
    outs = []
    for blk in range(s // BLOCK):
        start = blk * BLOCK
        end = start + BLOCK
        z = jnp.einsum('bqhd,bkhd->bhqk', q[:, start:end], k[:, :end],
                       preferred_element_type=jnp.float32) * scale
        t_idx = start + jnp.arange(BLOCK)[:, None]
        s_idx = jnp.arange(end)[None, :]
        strict = s_idx < t_idx
        log_beta = jax.nn.log_sigmoid(z)
        log_1mb = jnp.where(strict, jax.nn.log_sigmoid(-z), 0.0)
        after = lax.cumsum(log_1mb, axis=3, reverse=True) - log_1mb
        att = jnp.where(strict, jnp.exp(log_beta + after), 0.0)
        outs.append(jnp.einsum('bhqk,bkhd->bqhd', att, v[:, :end].astype(jnp.float32)))
    y = jnp.concatenate(outs, axis=1)
    return y.reshape(b, s, D_ATTN).astype(hn.dtype) @ w_out

def swiglu(hn, w_gate_up, w_down):
    g, u = jnp.split(hn @ w_gate_up, 2, axis=-1)
    return (jax.nn.silu(g) * u) @ w_down

def moe_swiglu(hn, w_router, w_gate_up, w_down):
    logits = jnp.einsum('bsd,de->bse', hn, w_router, preferred_element_type=jnp.float32)
    top_val, top_idx = lax.top_k(logits, TOP_K)
    top_w = jax.nn.softmax(top_val, axis=-1)
    gates = jnp.sum(jax.nn.one_hot(top_idx, N_EXPERTS, dtype=jnp.float32) * top_w[..., None], axis=-2)
    y = jnp.zeros_like(hn)
    for e in range(N_EXPERTS):
        y = y + gates[..., e:e + 1].astype(hn.dtype) * swiglu(hn, w_gate_up[e], w_down[e])
    return y

def setup_inputs(seed: int = 0) -> dict:
    key = jax.random.key(seed)
    ks = jax.random.split(key, 14)
    n_a = (DEPTH + 1) // 2
    n_b = DEPTH // 2

    def w(k, shape, fan_in):
        return jax.random.normal(k, shape, jnp.float32) * (fan_in ** -0.5)

    return {
        'x': jax.random.normal(ks[0], (BATCH, SEQ, D_MODEL), jnp.float32),
        'mix_norm': 1.0 + 0.02 * jax.random.normal(ks[1], (DEPTH, D_MODEL), jnp.float32),
        'ffn_norm': 1.0 + 0.02 * jax.random.normal(ks[2], (DEPTH, D_MODEL), jnp.float32),
        'dil_w_in': w(ks[3], (n_a, D_MODEL, N_GROUPS * 3 * D_ATTN), D_MODEL),
        'dil_w_out': w(ks[4], (n_a, D_ATTN, D_MODEL), D_ATTN),
        'sb_w_qkv': w(ks[5], (n_b, D_MODEL, 3 * D_ATTN), D_MODEL),
        'sb_w_out': w(ks[6], (n_b, D_ATTN, D_MODEL), D_ATTN),
        'ffn_w_gate_up': w(ks[7], (n_a, D_MODEL, 2 * D_FF), D_MODEL),
        'ffn_w_down': w(ks[8], (n_a, D_FF, D_MODEL), D_FF),
        'moe_w_router': w(ks[9], (n_b, D_MODEL, N_EXPERTS), D_MODEL),
        'moe_w_gate_up': w(ks[10], (n_b, N_EXPERTS, D_MODEL, 2 * D_FF), D_MODEL),
        'moe_w_down': w(ks[11], (n_b, N_EXPERTS, D_FF, D_MODEL), D_FF),
        'final_norm': 1.0 + 0.02 * jax.random.normal(ks[12], (D_MODEL,), jnp.float32),
    }

def reference(x, mix_norm, ffn_norm, dil_w_in, dil_w_out, sb_w_qkv, sb_w_out,
              ffn_w_gate_up, ffn_w_down, moe_w_router, moe_w_gate_up, moe_w_down, final_norm):
    slopes = alibi_slopes(N_HEADS)
    h = x
    for i in range(DEPTH):
        j = i // 2
        hn = rmsnorm(h, mix_norm[i])
        if i % N_MIXERS == 0:
            h = h + dilated_mixer(hn, dil_w_in[j], dil_w_out[j], slopes)
        else:
            h = h + stick_breaking_mixer(hn, sb_w_qkv[j], sb_w_out[j])
        hn = rmsnorm(h, ffn_norm[i])
        if i % 2 == 0:
            h = h + swiglu(hn, ffn_w_gate_up[j], ffn_w_down[j])
        else:
            h = h + moe_swiglu(hn, moe_w_router[j], moe_w_gate_up[j], moe_w_down[j])
    return rmsnorm(h, final_norm)


_drawn_inputs = setup_inputs


def setup_inputs(seed=0):
    import zlib

    import numpy as np

    out = dict(_drawn_inputs(seed))
    spreads = {}
    factors = {}
    for name, (base, spread) in spreads.items():
        noise = np.random.default_rng([zlib.crc32(name.encode()), seed]).standard_normal(out[name].shape)
        drawn = base * np.exp(spread * noise) if base else spread * noise
        out[name] = __import__('jax').numpy.asarray(drawn.astype(out[name].dtype))
    for name, factor in factors.items():
        out[name] = (out[name] * factor).astype(out[name].dtype)
    return out
```

```python
import numpy as np
import concourse.bass as bass
from concourse import mybir
from concourse.alu_op_type import AluOpType as ALU
from contextlib import ExitStack

F32 = mybir.dt.float32
F32R = mybir.dt.float32r
I32 = mybir.dt.int32
ACT = mybir.ActivationFunctionType
AX = mybir.AxisListType

P = 128
T = 256
TT = T // P
D = 1024
KT = D // P
H, DH = 16, 64
G = 3
FF = 3584
NE = 8
QUARTERS, QH = 4, 4
QN = QH * DH
SEEN = 3 * P
EPS = 1e-6
MASKED = 1e30

SK, SN = 4, 512
RAW, SPLIT = 6, 3
GU_CHUNKS = FF // 256
DOWN_GROUPS = FF // (SK * P)
DIL_UNITS = 3 * G
SB_UNITS = 3
OUT_SLABS = 4
FFN_SLABS = 2 * GU_CHUNKS + 2 * DOWN_GROUPS
DENSE_SLABS = QUARTERS * (DIL_UNITS + SB_UNITS) + 2 * OUT_SLABS + FFN_SLABS


def adjacent_tile(k):
    return slice((k // SK) * SK * P + k % SK, (k // SK + 1) * SK * P, SK)


def plain_tile(k):
    return slice(k * P, (k + 1) * P)


HEADS_AFTER = {3: [0], 4: [1, 2], 5: [3], 6: [4], 7: [5, 6], 8: [7], 9: [8], 10: [9, 10], 11: [11]}


class Count:

    def __init__(self, sem, start=0):
        self.sem, self.n, self.turn, self.per = sem, start, None, 0

    def step(self, by=1):
        self.n += by
        return by

    def enter(self, turn, per):
        assert self.turn is None
        self.turn, self.per, self.first = turn, per, self.n

    def leave(self, turns):
        assert self.n - self.first == self.per, (self.sem, self.n - self.first, self.per)
        if isinstance(turns, int):
            self.turn, self.n = None, self.first + turns * self.per
        else:
            self.turn, self.n = turns, self.first

    def now(self, back=0):
        v = self.n - back
        return v if self.turn is None else self.turn * self.per + v


class Slabs:

    def __init__(self):
        self.s = 0

    def next(self):
        s, self.s = self.s, self.s + 1
        return s % RAW, s % SPLIT


def trunk(nc, x, mix_norm, ffn_norm, dil_w_in, dil_w_out, sb_w_qkv, sb_w_out, ffn_w_gate_up, ffn_w_down,
          moe_w_router, moe_w_gate_up, moe_w_down, final_norm, out):
    ctx = ExitStack()
    with ctx:
        at = [nc.sbuf_base + (-nc.sbuf_base) % 64]

        def place(name, shape, dt=F32, offset=None):
            size = int(np.prod(shape[1:])) * 4
            if offset is None:
                offset, at[0] = at[0], at[0] + size + (-size) % 64
            return nc.alloc_sbuf_tensor_at(name, shape, dt, offset=offset)

        raw = place("raw", [P, RAW, SK, SN])
        w_hi = place("w_hi", [P, SPLIT, SK, SN], F32R)
        w_lo = place("w_lo", [P, SPLIT, SK, SN], F32R)
        h = place("h", [P, TT, D])
        hn = place("hn", [P, TT, D])
        x_hi = place("x_hi", [P, KT, T], F32R)
        x_lo_at = at[0]
        x_lo = place("x_lo", [P, KT, T], F32R)
        squares = place("squares", [P, TT, D], offset=x_lo_at)
        gains = place("gains", [P, 2, D])
        ident = place("ident", [P, P])
        ones = place("ones", [P, P])
        before = place("before", [P, P])
        from_on = place("from_on", [P, P])
        slot_no = place("slot_no", [P, P])
        negslope = place("negslope", [P, H])
        ssq = place("ssq", [P, TT])
        rstd = place("rstd", [P, TT])
        mean = place("mean", [P, TT])
        guess = place("guess", [P, TT], I32)
        newton = place("newton", [P, TT])
        region = at[0]

        a_qT = place("a_qT", [P, 2, G, 2 * T])
        a_kT = place("a_kT", [P, 2, G, 2 * T])
        a_v = place("a_v", [P, 2, G, TT * QN])
        a_s = place("a_s", [P, 2, G, SEEN])
        a_pT = place("a_pT", [P, 2, SEEN])
        dist = place("dist", [P, G, SEEN])
        d_int = place("d_int", [P, SEEN], I32)
        nmax = place("nmax", [P, 2, TT])
        zsum = place("zsum", [P, 2, TT])
        zinv = place("zinv", [P, TT])
        ends = [at[0]]

        at[0] = region
        f_hi = place("f_hi", [P, FF // P, T], F32R)
        f_lo = place("f_lo", [P, FF // P, T], F32R)
        f_sg = place("f_sg", [P, 2, 512])
        f_h = place("f_h", [P, 2, 512])
        ends.append(at[0])

        at[0] = region
        b_qT = place("b_qT", [P, H // 2, T])
        b_kT = place("b_kT", [P, H // 2, T])
        b_v = place("b_v", [P, QUARTERS, TT * QN])
        y_hi = place("y_hi", [P, KT, T], F32R)
        y_lo = place("y_lo", [P, KT, T], F32R)
        b_l = place("b_l", [P, 2, 3 * P])
        b_sp = place("b_sp", [P, 2, 3 * P])
        b_z = place("b_z", [P, 2, 3 * P])
        b_att = place("b_att", [P, 2, 3 * P])
        keep = place("keep", [P, 3 * P])
        hide = place("hide", [P, 3 * P])
        ends.append(at[0])

        at[0] = region
        m_hi = place("m_hi", [P, FF // P, P], F32R)
        m_lo = place("m_lo", [P, FF // P, P], F32R)
        g_hi = place("g_hi", [P, KT, P], F32R)
        g_lo = place("g_lo", [P, KT, P], F32R)
        m_sg = place("m_sg", [P, 2, 256])
        m_h = place("m_h", [P, 2, 256])
        yg = place("yg", [P, D])
        pick = place("pick", [P, TT, P])
        pick_w = place("pick_w", [P, TT, P])
        put_w = place("put_w", [P, TT * P])
        w_rt = place("w_rt", [P, KT, NE])
        names = ["lg", "eq", "cand", "one1", "one2", "lg2", "took", "gate", "tmp", "rev", "rank"]
        r = {n: place("r_" + n, [P, TT, NE]) for n in names}
        small = {n: place("r_" + n, [P, TT]) for n in ["m1", "c1", "m2", "c2", "d", "e", "den", "w1", "w2"]}
        slot_of = place("slot_of", [P, TT, 2 * NE + 1])
        gate_of = place("gate_of", [P, TT, 2 * NE + 1])
        counts = place("counts", [P, NE])
        most = place("most", [P, 1])
        turns_f = place("turns_f", [P, 1])
        turns_i = place("turns_i", [P, 1], I32)
        ends.append(at[0])
        assert max(ends) <= nc.sbuf_usable_end, (ends, nc.sbuf_usable_end)

        bank = [ctx.enter_context(nc.psum_tensor(f"bank{b}", [P, 512], F32)) for b in range(8)]

        def sem(name):
            return ctx.enter_context(nc.semaphore(name))

        raw_full = [sem(f"raw_full{i}") for i in range(RAW)]
        s_hi = sem("hi_made")
        s_split = sem("split_made")
        s_free = sem("split_free")
        s_x = sem("x_loaded")
        s_gain = [sem(f"gain_loaded{i}") for i in range(2)]
        s_const = sem("const_made")
        s_dint = sem("dint_used")
        s_dmask = sem("dmask_made")
        s_ssq = sem("ssq_made")
        s_nstep = sem("norm_step")
        s_hn = sem("hn_made")
        s_xT = sem("xT_made")
        s_xhi = sem("xhi_made")
        s_xlo = sem("xlo_made")
        s_qkv = sem("qkv_read")
        s_h = sem("h_made")
        s_scores = sem("scores_made")
        s_scread = sem("scores_read")
        s_max = sem("max_made")
        s_exp = sem("exp_made")
        s_pT = sem("pT_made")
        s_pTread = sem("pT_read")
        s_pv = sem("pv_made")
        s_zinv = sem("zinv_made")
        s_y = sem("y_made")
        s_silu = sem("silu_made")
        s_gu = sem("gu_read")
        s_fhi = sem("f_hi_made")
        s_flo = sem("f_lo_made")
        s_z = sem("z_made")
        s_zread = sem("z_read")
        s_astep = sem("act_step")
        s_sp = sem("sp_made")
        s_spm = sem("sp_masked")
        s_cum = sem("cum_made")
        s_arg = sem("arg_made")
        s_att = sem("att_made")
        s_o = sem("o_made")
        s_ohi = sem("o_hi_made")
        s_olo = sem("o_lo_made")
        s_wrt = sem("router_loaded")
        s_lg = sem("logits_made")
        s_rstep = sem("route_step")
        s_took = sem("took_made")
        s_e2 = sem("gate_exp_made")
        s_rank = sem("rank_made")
        s_routed = sem("routed")
        s_clear = sem("cleared")
        s_pick = sem("pick_made")
        s_xg = sem("gathered")
        s_ghi = sem("g_hi_made")
        s_glo = sem("g_lo_made")
        s_msilu = sem("expert_silu_made")
        s_mread = sem("expert_gu_read")
        s_mT = sem("expert_hT_made")
        s_mhi = sem("m_hi_made")
        s_mlo = sem("m_lo_made")
        s_yread = sem("expert_y_read")
        s_pickw = sem("pick_w_made")
        s_putT = sem("put_made")
        s_put = sem("put_read")
        s_scat = sem("scattered")
        s_added = sem("added")
        s_out = sem("out_stored")

        ITEM = {s_hi: FFN_SLABS, s_split: FFN_SLABS, s_free: FFN_SLABS, s_pick: 1, s_xg: 2, s_ghi: 2, s_glo: 2,
                s_msilu: GU_CHUNKS, s_mread: GU_CHUNKS, s_mT: GU_CHUNKS, s_mhi: GU_CHUNKS,
                s_mlo: GU_CHUNKS, s_yread: 1, s_pickw: 1, s_putT: 1, s_put: 1, s_scat: 4, s_added: 4}

        def counts_of():
            class Counts(dict):
                def __missing__(self, s):
                    self[s] = Count(s, {s_split: RAW, s_free: SPLIT}.get(s, 0))
                    return self[s]

                def enter(self, per, turn):
                    for s, n in per.items():
                        self[s].enter(turn, n)

                def leave(self, per, turns, used):
                    for s, n in per.items():
                        if s not in used:
                            self[s].n = self[s].first + n
                        self[s].leave(turns)
            return Counts()

        block = ctx.enter_context(nc.Block())

        @block.sync
        def _(sp):
            slabs = Slabs()
            free = Count(s_split)

            def load(src, narrow=False):
                slot, _ = slabs.next()
                free.step()
                sp.wait_ge(s_split, free.now())
                dst = raw[:, slot].rearrange("p k (a n) -> p (k a) n", a=2) if narrow else raw[:, slot]
                sp.dma_start(dst, src).then_inc(raw_full[slot], 16)

            def square(w, kh, cols):
                return w[kh * SK * P:(kh + 1) * SK * P, cols].rearrange("(k p) n -> p k n", p=P)

            def load_out(w):
                for ch in range(2):
                    for kh in range(2):
                        load(square(w, kh, slice(ch * SN, (ch + 1) * SN)))

            def load_unit(w, col):
                load(w[:, col:col + QN].rearrange("(k p) n -> p k n", p=P), True)

            def load_gate_up(w):
                for j in range(GU_CHUNKS):
                    for kh in range(2):
                        v = w[kh * SK * P:(kh + 1) * SK * P, :]
                        v = v.rearrange("(p k) (a f) -> p (k a) f", p=P, a=2)
                        load(v[:, :, j * 256:(j + 1) * 256], True)

            def load_down(w):
                for kg in range(DOWN_GROUPS):
                    for half in range(2):
                        load(square(w, kg, slice(half * SN, (half + 1) * SN)))

            sp.dma_start(h[:, :, :], x[0].rearrange("(t p) d -> p t d", p=P)).then_inc(s_x, 16)
            for q in range(QUARTERS):
                for u in range(DIL_UNITS):
                    load_unit(dil_w_in[0], u * D + q * QN)
            load_out(dil_w_out[0])
            load_gate_up(ffn_w_gate_up[0])
            load_down(ffn_w_down[0])
            for q in range(QUARTERS):
                for u in range(SB_UNITS):
                    load_unit(sb_w_qkv[0], u * D + q * QN)
            load_out(sb_w_out[0])

            def load_expert(e):
                load_gate_up(moe_w_gate_up[0, bass.ds(e, 1)].squeeze(0))
                load_down(moe_w_down[0, bass.ds(e, 1)].squeeze(0))

            with sp.Fori(0, NE) as e:
                free.enter(e, FFN_SLABS)
                load_expert(e)
                free.leave(NE)
            sp.wait_ge(s_routed, 1)
            turns = sp.value_load(turns_i[0:1, 0:1], min_val=NE, max_val=2 * NE)
            with sp.If(turns > NE):
                with sp.Fori(0, NE) as e:
                    free.enter(e, FFN_SLABS)
                    load_expert(e)
                    free.leave(NE)
            with sp.Else():
                pass
            sp.wait_ge(s_hn, 10)
            sp.dma_start(out[0].rearrange("(t p) d -> p t d", p=P), hn[:, :, :]).then_inc(s_out, 16)
            sp.wait_ge(s_out, 16)

        @block.gpsimd
        def _(pool):
            def gain(n, row):
                pool.dma_start(gains[:, n % 2], row.partition_broadcast(P)).then_inc(s_gain[n % 2], 16)

            gain(0, mix_norm[0])
            gain(1, ffn_norm[0])
            nc.gpsimd.memset(ones[:, :], 1.0)
            nc.gpsimd.memset(ident[:, :], 0.0)
            for hd in range(H):
                nc.gpsimd.memset(negslope[:, hd:hd + 1], -(2.0 ** (-8.0 * (hd + 1) / H)))
            nc.gpsimd.iota(slot_no[:, :], [[1, P]], base=0, channel_multiplier=0,
                           allow_small_or_imprecise_dtypes=True)
            for k0, n, base in ((0, P, 0), (P, T, P)):
                nc.gpsimd.iota(d_int[:, k0:k0 + n], [[-1, n]], base=base, channel_multiplier=1)
                ins = nc.gpsimd.iota(dist[:, 0, k0:k0 + n], [[-1, n]], base=base, channel_multiplier=1,
                                     allow_small_or_imprecise_dtypes=True)
            ins.then_inc(s_const, 1)
            pool.wait_ge(s_const, 1)
            nc.gpsimd.affine_select(out=ident[:, :], in_=ident[:, :], compare_op=ALU.not_equal, fill=1.0,
                                    base=0, pattern=[[-1, P]], channel_multiplier=1)
            nc.gpsimd.affine_select(out=before[:, :], in_=ones[:, :], compare_op=ALU.is_ge, fill=0.0,
                                    base=-1, pattern=[[1, P]], channel_multiplier=-1)
            nc.gpsimd.affine_select(out=from_on[:, :], in_=ones[:, :], compare_op=ALU.is_ge, fill=0.0,
                                    base=0, pattern=[[-1, P]], channel_multiplier=1).then_inc(s_const, 1)
            pool.wait_ge(s_dint, 6)
            for k0, n, base in ((0, P, 0), (P, T, P)):
                ins = nc.gpsimd.affine_select(out=dist[:, 0, k0:k0 + n], in_=dist[:, 0, k0:k0 + n],
                                              compare_op=ALU.is_ge, fill=MASKED, base=P - base, pattern=[[1, n]],
                                              channel_multiplier=-1)
            ins.then_inc(s_dmask, 1)
            pool.wait_ge(s_dmask, 1)
            for g in range(G):
                for k0, n, base in ((0, P, 0), (P, T, P)):
                    ins = nc.gpsimd.affine_select(out=dist[:, g, k0:k0 + n], in_=dist[:, g, k0:k0 + n],
                                                  compare_op=ALU.is_ge, fill=MASKED, base=base, pattern=[[-1, n]],
                                                  channel_multiplier=1)
            ins.then_inc(s_dmask, 1)
            pool.wait_ge(s_hn, 2)
            gain(2, mix_norm[1])
            for j in range(GU_CHUNKS):
                pool.wait_ge(s_fhi, j + 1)
                nc.gpsimd.tensor_tensor(f_lo[:, 2 * j:2 * j + 2].rearrange("p a t -> p (a t)"), f_h[:, j % 2],
                                        f_hi[:, 2 * j:2 * j + 2].rearrange("p a t -> p (a t)").bitcast(F32),
                                        ALU.subtract).then_inc(s_flo, 1)
                if j == 0:
                    gain(3, ffn_norm[1])
            pool.wait_ge(s_h, 3)
            nc.gpsimd.memset(keep[:, :], 1.0)
            nc.gpsimd.memset(hide[:, :], 0.0).then_inc(s_const, 1)
            pool.wait_ge(s_const, 3)
            for c0, n in ((0, T), (T, P)):
                for m, fill in ((keep, 0.0), (hide, -MASKED)):
                    nc.gpsimd.affine_select(out=m[:, c0:c0 + n], in_=m[:, c0:c0 + n], compare_op=ALU.is_ge,
                                            fill=fill, base=-1, pattern=[[1, n]],
                                            channel_multiplier=-1).then_inc(s_const, 1)
            pool.wait_ge(s_const, 7)
            for i in range(H):
                pool.wait_ge(s_sp, i + 1)
                nc.gpsimd.tensor_tensor(b_sp[:, i % 2], b_sp[:, i % 2], keep[:, :], ALU.mult).then_inc(s_spm, 1)
                if i == 0:
                    gain(4, final_norm)
            pool.wait_ge(s_h, 5)
            pool.dma_start(w_rt[:, :, :].rearrange("p (a k) e -> p a k e", a=2), moe_w_router[0].rearrange("(a p k) e -> p a k e", p=P, k=SK)).then_inc(s_wrt, 16)
            nc.gpsimd.memset(yg[:, :], 0.0)
            nc.gpsimd.memset(slot_of[:, :, :], -1.0)
            nc.gpsimd.memset(gate_of[:, :, :], 0.0)
            nc.gpsimd.iota(r["rev"][:, :, :], [[0, TT], [-1, NE]], base=NE, channel_multiplier=0,
                           allow_small_or_imprecise_dtypes=True)
            nc.gpsimd.memset(put_w[:, :], 0.0).then_inc(s_clear, 1)

        @block.scalar
        def _(act):
            slabs, c = Slabs(), counts_of()
            filled = [Count(s) for s in raw_full]
            done = Count(s_free, SPLIT)

            def hi():
                a, b = slabs.next()
                filled[a].step(16)
                act.wait_ge(raw_full[a], filled[a].now())
                c[s_free].step()
                act.wait_ge(s_free, c[s_free].now())
                nc.scalar.activation(w_hi[:, b], raw[:, a], ACT.Copy).then_inc(s_hi, c[s_hi].step())

            c[s_free].n = 0

            def norm():
                c[s_ssq].step()
                for t in range(TT):
                    ins = nc.scalar.activation(squares[:, t], h[:, t], ACT.Square, accum_out=ssq[:, t:t + 1])
                ins.then_inc(s_ssq, 1)

            def x_hi_parts():
                for b in range(4):
                    c[s_xT].step()
                    act.wait_ge(s_xT, c[s_xT].now())
                    nc.scalar.activation(
                        x_hi[:, 2 * b:2 * b + 2].rearrange("p k t -> p (k t)"), bank[b][:, :], ACT.Copy).then_inc(s_xhi, c[s_xhi].step())

            def ahead():
                if slabs.s < DENSE_SLABS:
                    hi()

            def y_hi_parts():
                c[s_xT].step()
                b = (c[s_xT].n - 1) % 4
                act.wait_ge(s_xT, c[s_xT].now())
                nc.scalar.activation(x_hi[:, 2 * b:2 * b + 2].rearrange("p k t -> p (k t)"), bank[(0, 1, 0, 2)[b]][:, :],
                                     ACT.Copy).then_inc(s_xhi, c[s_xhi].step())

            act.wait_ge(s_x, 16)
            norm()
            ahead()
            ahead()
            x_hi_parts()

            def keep_unit(dst, scale):
                done.step()
                act.wait_ge(s_free, done.now())
                nc.scalar.activation(dst, bank[(done.n - SPLIT - 1) % 2][:, :], ACT.Copy,
                                     scale=scale).then_inc(s_qkv, c[s_qkv].step())

            def probabilities(n):
                act.wait_ge(s_max, n + 1)
                for qt, cols in enumerate((slice(0, P), slice(P, SEEN))):
                    ins = nc.scalar.activation(a_s[:, n % 2, :, cols], a_s[:, n % 2, :, cols], ACT.Exp,
                                               bias=nmax[:, n % 2, qt:qt + 1], accum_out=zsum[:, n % 2, qt:qt + 1])
                ins.then_inc(s_exp, 1)

            def keep_transposed(n):
                for g in range(G):
                    m = n * G + g
                    act.wait_ge(s_pT, m + 1)
                    if m >= 2:
                        act.wait_ge(s_pv, m - 1)
                    nc.scalar.activation(a_pT[:, m % 2], bank[5 + m % 2][:, 0:SEEN], ACT.Copy).then_inc(s_pTread, 1)

            for q in range(QUARTERS + 1):
                for u in range(DIL_UNITS):
                    if q < QUARTERS:
                        ahead()
                        g, part = divmod(u, 3)
                        if q >= 2 and u == 0:
                            act.wait_ge(s_pv, (q - 1) * QH * G)
                        keep_unit((a_qT, a_kT, a_v)[part][:, q % 2, g], DH ** -0.5 if part == 0 else 1.0)
                    if q == 0:
                        continue
                    n = (q - 1) * QH + u // 2
                    if u == 0:
                        probabilities(n)
                    elif u % 2 == 1:
                        keep_transposed(n)
                    elif u // 2 < QH:
                        probabilities(n)
                    if q == QUARTERS and u in (0, 2):
                        for _ in range(2 if u == 0 else 1):
                            y_hi_parts()
            ahead()
            y_hi_parts()
            for _ in range(OUT_SLABS - 1):
                ahead()
            done.step(OUT_SLABS)

            act.wait_ge(s_h, 2)
            norm()
            x_hi_parts()

            def gate(j):
                done.step(2)
                act.wait_ge(s_free, done.now())
                if j >= 2:
                    act.wait_ge(s_gu, j - 1)
                nc.scalar.activation(f_sg[:, j % 2], bank[4 + 2 * (j % 2)][:, :], ACT.Silu).then_inc(s_silu, 1)
                act.wait_ge(s_gu, j + 1)
                nc.scalar.activation(f_hi[:, 2 * j:2 * j + 2].rearrange("p a t -> p (a t)"), f_h[:, j % 2],
                                     ACT.Copy).then_inc(s_fhi, 1)

            for j in range(GU_CHUNKS):
                ahead()
                ahead()
                gate(j)
            for _ in range(2 * DOWN_GROUPS):
                ahead()
            done.step(2 * DOWN_GROUPS)

            act.wait_ge(s_h, 3)
            norm()
            x_hi_parts()

            nc.scalar.preload_act_table_set("natural_log_exp_and_others")
            step = Count(s_astep)

            def log_part(n):
                act.wait_ge(s_z, n + 1)
                if n >= 2:
                    act.wait_ge(s_sp, n - 1)
                nc.scalar.activation(b_l[:, n % 2], bank[2 + n % 2][:, 0:SEEN], ACT.Abs).then_inc(s_astep, step.step())
                act.wait_ge(s_astep, step.now())
                nc.scalar.activation(b_l[:, n % 2], b_l[:, n % 2], ACT.Exp, scale=-1.0).then_inc(s_astep, step.step())
                act.wait_ge(s_astep, step.now())
                nc.scalar.activation(b_l[:, n % 2], b_l[:, n % 2], ACT.Ln, bias=1.0).then_inc(s_astep, step.step())

            def head_slot(n):
                if n < H:
                    log_part(n)
                if 0 <= n - 1 < H:
                    m = n - 1
                    act.wait_ge(s_arg, m + 1)
                    if m >= 2:
                        act.wait_ge(s_o, m - 1)
                    nc.scalar.activation(b_att[:, m % 2], b_z[:, m % 2], ACT.Exp).then_inc(s_att, 1)
                if n - 2 >= 0 and n % 2 == 1:
                    m = n - 2
                    act.wait_ge(s_o, m + 1)
                    nc.scalar.activation(y_hi[:, m // 2], bank[6 + m // 2 % 2][:, 0:T], ACT.Copy).then_inc(s_ohi, 1)

            for q in range(QUARTERS):
                for u in range(SB_UNITS):
                    ahead()
                    dst = (b_qT[:, 2 * q:2 * q + 2].rearrange("p b t -> p (b t)"),
                           b_kT[:, 2 * q:2 * q + 2].rearrange("p b t -> p (b t)"), b_v[:, q])[u]
                    keep_unit(dst, DH ** -0.5 if u == 0 else 1.0)
                    for n in HEADS_AFTER.get(q * SB_UNITS + u, []):
                        head_slot(n)
            head_slot(12)
            ahead()
            for n in range(13, H + 2):
                head_slot(n)
            for _ in range(OUT_SLABS - 1):
                ahead()
            done.step(OUT_SLABS)

            act.wait_ge(s_h, 5)
            norm()
            x_hi_parts()
            act.wait_ge(s_took, 1)
            nc.scalar.activation(small["e"][:, :], small["d"][:, :], ACT.Exp).then_inc(s_e2, 1)
            act.wait_ge(s_routed, 1)
            turns = act.value_load(turns_i[0:1, 0:1], min_val=NE, max_val=2 * NE)

            def tokens_hi():
                for b in range(2):
                    c[s_xg].step()
                    act.wait_ge(s_xg, c[s_xg].now())
                    nc.scalar.activation(
                        g_hi[:, 4 * b:4 * b + 4].rearrange("p k s -> p (k s)"), bank[6 + b][:, :], ACT.Copy).then_inc(s_ghi, c[s_ghi].step())

            tokens_hi()
            with act.Fori(0, turns) as item:
                c.enter(ITEM, item)
                done.enter(item, FFN_SLABS)
                for f in filled:
                    f.enter(item, 16 * FFN_SLABS // RAW)

                def silu(j):
                    done.step(2)
                    act.wait_ge(s_free, done.now())
                    act.wait_ge(s_mread, c[s_mread].now(1 if j >= 2 else 0))
                    nc.scalar.activation(m_sg[:, j % 2], bank[j % 2][:, 0:256], ACT.Silu).then_inc(s_msilu, c[s_msilu].step())
                    c[s_mread].step()

                def hidden_hi(j):
                    c[s_mT].step()
                    act.wait_ge(s_mT, c[s_mT].now())
                    nc.scalar.activation(m_hi[:, 2 * j:2 * j + 2].rearrange("p a s -> p (a s)"),
                                                         bank[2 + j % 2][:, 0:256], ACT.Copy).then_inc(s_mhi, c[s_mhi].step())

                for j in range(GU_CHUNKS):
                    hi()
                    hi()
                    if j >= 1:
                        silu(j - 1)
                    if j >= 2:
                        hidden_hi(j - 2)
                    if j == 6:
                        c[s_putT].step()
                        act.wait_ge(s_putT, c[s_putT].now())
                        nc.scalar.activation(put_w[:, :], bank[6][:, 0:T], ACT.Copy).then_inc(s_put, c[s_put].step())
                for kg in range(DOWN_GROUPS):
                    hi()
                    hi()
                    if kg == 0:
                        silu(GU_CHUNKS - 1)
                        hidden_hi(GU_CHUNKS - 2)
                    if kg == 1:
                        hidden_hi(GU_CHUNKS - 1)
                    if kg == 4:
                        tokens_hi()
                done.step(2 * DOWN_GROUPS)
                act.wait_ge(s_free, done.now())
                for n in range(2):
                    ins = nc.scalar.activation(yg[:, n * SN:(n + 1) * SN], bank[4 + n][:, :], ACT.Copy)
                ins.then_inc(s_yread, c[s_yread].step())
                c.leave(ITEM, turns, {s_hi, s_free, s_mread, s_msilu, s_mT, s_mhi, s_putT, s_put, s_xg,
                                      s_ghi, s_yread})
                done.leave(turns)
                for f in filled:
                    f.leave(turns)
            c[s_added].step(4)
            act.wait_ge(s_added, c[s_added].now())
            norm()

        @block.vector
        def _(dve):
            slabs, c = Slabs(), counts_of()
            done = Count(s_free, SPLIT)

            def lo():
                a, b = slabs.next()
                c[s_hi].step()
                dve.wait_ge(s_hi, c[s_hi].now())
                nc.vector.tensor_tensor(w_lo[:, b], raw[:, a], w_hi[:, b].bitcast(F32),
                                                          ALU.subtract).then_inc(s_split, c[s_split].step())

            n_norm = [0]
            steps = Count(s_nstep)

            def inverse_root():
                def link(ins):
                    ins.then_inc(s_nstep, steps.step())
                    dve.wait_ge(s_nstep, steps.now())

                link(nc.vector.tensor_scalar(mean[:, :], ssq[:, :], 1.0 / D, EPS, ALU.mult, ALU.add))
                link(nc.vector.tensor_scalar(guess[:, :], mean[:, :].bitcast(I32), 1, None, ALU.logical_shift_right))
                link(nc.vector.tensor_scalar(rstd[:, :].bitcast(I32), guess[:, :], -1.0, float(0x5F3759DF), ALU.mult,
                                             ALU.add))
                for _ in range(3):
                    link(nc.vector.tensor_tensor(newton[:, :], rstd[:, :], rstd[:, :], ALU.mult))
                    link(nc.vector.tensor_tensor(newton[:, :], newton[:, :], mean[:, :], ALU.mult))
                    link(nc.vector.tensor_scalar(newton[:, :], newton[:, :], -0.5, 1.5, ALU.mult, ALU.add))
                    link(nc.vector.tensor_tensor(rstd[:, :], rstd[:, :], newton[:, :], ALU.mult))

            def norm():
                n = n_norm[0]
                n_norm[0] += 1
                dve.wait_ge(s_ssq, n + 1)
                inverse_root()
                dve.wait_ge(s_gain[n % 2], 16 * (n // 2 + 1))
                for half in range(2):
                    cols = slice(half * SN, (half + 1) * SN)
                    for t in range(TT):
                        ins = nc.vector.scalar_tensor_tensor(out=hn[:, t, cols], in0=h[:, t, cols],
                                                             scalar=rstd[:, t:t + 1], in1=gains[:, n % 2, cols],
                                                             op0=ALU.mult, op1=ALU.mult)
                    ins.then_inc(s_hn, 1)

            def x_lo_parts():
                for b in range(4):
                    k = slice(2 * b, 2 * b + 2)
                    c[s_xhi].step()
                    dve.wait_ge(s_xhi, c[s_xhi].now())
                    nc.vector.tensor_tensor(x_lo[:, k].rearrange("p k t -> p (k t)"), bank[b][:, :],
                                            x_hi[:, k].rearrange("p k t -> p (k t)").bitcast(F32),
                                            ALU.subtract).then_inc(s_xlo, 1)

            def add_chunk(ch):
                done.step(2)
                dve.wait_ge(s_free, done.now())
                for t in range(TT):
                    cols = slice(ch * SN, (ch + 1) * SN)
                    ins = nc.vector.tensor_tensor(h[:, t, cols], h[:, t, cols], bank[3 * ch + t][:, :], ALU.add)
                ins.then_inc(s_h, 1)

            def ahead():
                if slabs.s < DENSE_SLABS:
                    lo()

            def y_lo_parts():
                c[s_xhi].step()
                b = (c[s_xhi].n - 1) % 4
                k = slice(2 * b, 2 * b + 2)
                dve.wait_ge(s_xhi, c[s_xhi].now())
                nc.vector.tensor_tensor(x_lo[:, k].rearrange("p k t -> p (k t)"), bank[(0, 1, 0, 2)[b]][:, :],
                                        x_hi[:, k].rearrange("p k t -> p (k t)").bitcast(F32),
                                        ALU.subtract).then_inc(s_xlo, 1)

            nc.vector.sem_inc(s_split, RAW)
            dve.wait_ge(s_const, 1)
            for g, stride in ((1, 4), (2, 16)):
                m = a_s[:, 0, g - 1].bitcast(I32)
                nc.vector.tensor_scalar(m, d_int[:, :], stride - 1, None, ALU.bitwise_and).then_inc(s_dint, 1)
                dve.wait_ge(s_dint, 3 * (g - 1) + 1)
                nc.vector.tensor_scalar(a_s[:, 1, g - 1], m, 0.0, MASKED, ALU.not_equal,
                                        ALU.mult).then_inc(s_dint, 1)
                dve.wait_ge(s_dint, 3 * (g - 1) + 2)
                nc.vector.tensor_tensor(dist[:, g], a_s[:, 1, g - 1], dist[:, 0],
                                        ALU.add).then_inc(s_dint, 1)
            norm()
            ahead()
            ahead()
            x_lo_parts()
            dve.wait_ge(s_dmask, 2)

            def bias_scores(n):
                for g in range(G):
                    m = n * G + g
                    dve.wait_ge(s_scores, m + 1)
                    if n >= 2:
                        dve.wait_ge(s_pT, (n - 1) * G)
                    nc.vector.scalar_tensor_tensor(out=a_s[:, n % 2, g], in0=dist[:, g], scalar=negslope[:, n:n + 1],
                                                   in1=bank[2 + g][:, 0:SEEN], op0=ALU.mult,
                                                   op1=ALU.add).then_inc(s_scread, 1)
                dve.wait_ge(s_scread, (n + 1) * G)
                for qt, cols in enumerate((slice(0, P), slice(P, SEEN))):
                    ins = nc.vector.tensor_reduce(nmax[:, n % 2, qt:qt + 1], a_s[:, n % 2, :, cols], AX.XY, ALU.max,
                                                  negate=True)
                ins.then_inc(s_max, 1)

            def finish_head(n):
                dve.wait_ge(s_pv, (n + 1) * G)
                nc.vector.reciprocal(zinv[:, :], zsum[:, n % 2]).then_inc(s_zinv, 1)
                dve.wait_ge(s_zinv, n + 1)
                nc.vector.tensor_tensor(hn[:, :, n * DH:(n + 1) * DH],
                                        bank[7][:, 0:TT * DH].rearrange("p (a d) -> p a d", a=TT),
                                        zinv[:, :].unsqueeze(2).to_broadcast([P, TT, DH]), ALU.mult).then_inc(s_y, 1)

            for q in range(QUARTERS + 1):
                for u in range(DIL_UNITS):
                    if q < QUARTERS:
                        ahead()
                    if q == 0:
                        continue
                    n = (q - 1) * QH + u // 2
                    if u == 0:
                        bias_scores(n)
                    elif u % 2 == 0:
                        finish_head(n - 1)
                    elif u // 2 < QH - 1:
                        bias_scores(n + 1)
                    if q == QUARTERS and u in (0, 2):
                        for _ in range(2 if u == 0 else 1):
                            y_lo_parts()
            ahead()
            y_lo_parts()
            for _ in range(OUT_SLABS - 1):
                ahead()
            done.step(QUARTERS * DIL_UNITS)
            for ch in range(2):
                add_chunk(ch)

            norm()
            x_lo_parts()

            def gated(j):
                dve.wait_ge(s_silu, j + 1)
                if j >= 2:
                    dve.wait_ge(s_flo, j - 1)
                nc.vector.tensor_tensor(f_h[:, j % 2], f_sg[:, j % 2], bank[4 + 2 * (j % 2) + 1][:, :],
                                        ALU.mult).then_inc(s_gu, 1)

            for j in range(GU_CHUNKS):
                ahead()
                ahead()
                gated(j)
            for _ in range(2 * DOWN_GROUPS):
                ahead()
            done.step(FFN_SLABS)
            dve.wait_ge(s_free, done.now())
            for t in range(TT):
                for n in range(2):
                    cols = slice(n * SN, (n + 1) * SN)
                    ins = nc.vector.tensor_tensor(h[:, t, cols], h[:, t, cols], bank[2 * t + n][:, :], ALU.add)
            ins.then_inc(s_h, 1)

            norm()
            x_lo_parts()
            dve.wait_ge(s_const, 7)

            def head_slot(n):
                if n < H:
                    dve.wait_ge(s_astep, 3 * (n + 1))
                    if n >= 2:
                        dve.wait_ge(s_cum, n - 1)
                    z = bank[2 + n % 2][:, 0:SEEN]
                    nc.vector.scalar_tensor_tensor(out=b_sp[:, n % 2], in0=z, scalar=0.0, in1=b_l[:, n % 2],
                                                   op0=ALU.max, op1=ALU.add).then_inc(s_sp, 1)
                    if n >= 2:
                        dve.wait_ge(s_att, n - 1)
                    nc.vector.tensor_tensor(b_z[:, n % 2], z, hide[:, :], ALU.add).then_inc(s_zread, 1)
                if 0 <= n - 1 < H:
                    m = n - 1
                    dve.wait_ge(s_zread, m + 1)
                    dve.wait_ge(s_cum, m + 1)
                    nc.vector.tensor_tensor(b_z[:, m % 2], b_z[:, m % 2], bank[4 + m % 2][:, 0:SEEN],
                                            ALU.subtract).then_inc(s_arg, 1)
                if n - 2 >= 0 and n % 2 == 1:
                    b = (n - 2) // 2
                    dve.wait_ge(s_ohi, b + 1)
                    nc.vector.tensor_tensor(y_lo[:, b], bank[6 + b % 2][:, 0:T], y_hi[:, b].bitcast(F32),
                                            ALU.subtract).then_inc(s_olo, 1)

            for q in range(QUARTERS):
                for u in range(SB_UNITS):
                    ahead()
                    for n in HEADS_AFTER.get(q * SB_UNITS + u, []):
                        head_slot(n)
            head_slot(12)
            ahead()
            for n in range(13, H + 2):
                head_slot(n)
            for _ in range(OUT_SLABS - 1):
                ahead()
            done.step(QUARTERS * SB_UNITS)
            for ch in range(2):
                add_chunk(ch)

            norm()
            x_lo_parts()
            route = Count(s_rstep)

            def link(ins):
                ins.then_inc(s_rstep, route.step())
                dve.wait_ge(s_rstep, route.now())

            def over_experts(v):
                return v[:, :].unsqueeze(2).to_broadcast([P, TT, NE])

            def first_of_max(lg, m, cand1, one):
                link(nc.vector.tensor_reduce(small[m][:, :], r[lg][:, :, :], AX.X, ALU.max))
                link(nc.vector.tensor_tensor(r["eq"][:, :, :], r[lg][:, :, :], over_experts(small[m]), ALU.is_equal))
                link(nc.vector.tensor_tensor(r["cand"][:, :, :], r["eq"][:, :, :], r["rev"][:, :, :], ALU.mult))
                link(nc.vector.tensor_reduce(small[cand1][:, :], r["cand"][:, :, :], AX.X, ALU.max))
                link(nc.vector.tensor_tensor(r[one][:, :, :], r["rev"][:, :, :], over_experts(small[cand1]),
                                             ALU.is_equal))

            dve.wait_ge(s_clear, 1)
            dve.wait_ge(s_lg, 1)
            link(nc.vector.tensor_copy(r["lg"][:, :, :].rearrange("p t e -> p (t e)"), bank[4][:, 0:TT * NE]))
            first_of_max("lg", "m1", "c1", "one1")
            link(nc.vector.scalar_tensor_tensor(out=r["lg2"][:, :, :], in0=r["one1"][:, :, :], scalar=-3e38,
                                                in1=r["lg"][:, :, :], op0=ALU.mult, op1=ALU.add))
            first_of_max("lg2", "m2", "c2", "one2")
            link(nc.vector.tensor_tensor(small["d"][:, :], small["m2"][:, :], small["m1"][:, :], ALU.subtract))
            nc.vector.tensor_tensor(r["took"][:, :, :], r["one1"][:, :, :], r["one2"][:, :, :],
                                    ALU.add).then_inc(s_took, 1)
            dve.wait_ge(s_e2, 1)
            link(nc.vector.tensor_scalar(small["den"][:, :], small["e"][:, :], 1.0, None, ALU.add))
            link(nc.vector.reciprocal(small["w1"][:, :], small["den"][:, :]))
            link(nc.vector.tensor_tensor(small["w2"][:, :], small["w1"][:, :], small["e"][:, :], ALU.mult))
            link(nc.vector.tensor_tensor(r["gate"][:, :, :], r["one1"][:, :, :], over_experts(small["w1"]), ALU.mult))
            link(nc.vector.tensor_tensor(r["tmp"][:, :, :], r["one2"][:, :, :], over_experts(small["w2"]), ALU.mult))
            for n in range(2):
                link(nc.vector.tensor_tensor(gate_of[:, :, n * NE:(n + 1) * NE], r["gate"][:, :, :], r["tmp"][:, :, :],
                                             ALU.add))
            dve.wait_ge(s_rank, 1)
            rank = bank[5][:, 0:TT * NE].rearrange("p (t e) -> p t e", t=TT)
            link(nc.vector.scalar_tensor_tensor(out=r["rank"][:, :, :], in0=rank, scalar=1.0, in1=r["took"][:, :, :],
                                                op0=ALU.add, op1=ALU.mult))
            link(nc.vector.tensor_scalar(slot_of[:, :, 0:NE], r["rank"][:, :, :], -1.0, None, ALU.add))
            link(nc.vector.tensor_scalar(slot_of[:, :, NE:2 * NE], r["rank"][:, :, :], -1.0 - P, None, ALU.add))
            link(nc.vector.tensor_reduce(most[:, :], bank[5][:, TT * NE:TT * NE + NE], AX.X, ALU.max))
            link(nc.vector.tensor_scalar(turns_f[:, :], most[:, :], float(P), float(NE), ALU.is_gt, ALU.mult))
            nc.vector.tensor_scalar(turns_i[:, :], turns_f[:, :], float(NE), None, ALU.add).then_inc(s_routed, 1)
            dve.wait_ge(s_routed, 1)
            turns = dve.value_load(turns_i[0:1, 0:1], min_val=NE, max_val=2 * NE)

            def pick_tokens(item):
                dve.wait_ge(s_xg, c[s_xg].now())
                for t in range(TT):
                    ins = nc.vector.tensor_scalar(pick[:, t], slot_no[:, :], slot_of[:, t, bass.ds(item, 1)], None,
                                                  ALU.is_equal)
                ins.then_inc(s_pick, c[s_pick].step())

            def tokens_lo():
                for b in range(2):
                    k = slice(4 * b, 4 * b + 4)
                    c[s_ghi].step()
                    dve.wait_ge(s_ghi, c[s_ghi].now())
                    nc.vector.tensor_tensor(
                        g_lo[:, k].rearrange("p k s -> p (k s)"), bank[6 + b][:, :],
                        g_hi[:, k].rearrange("p k s -> p (k s)").bitcast(F32), ALU.subtract).then_inc(s_glo, c[s_glo].step())

            def add_expert(t):
                for n in range(2):
                    cols = slice(n * SN, (n + 1) * SN)
                    c[s_scat].step()
                    dve.wait_ge(s_scat, c[s_scat].now())
                    nc.vector.tensor_tensor(h[:, t, cols], h[:, t, cols], bank[6 + n][:, :], ALU.add).then_inc(s_added, c[s_added].step())

            pick_tokens(0)
            c[s_xg].step(2)
            tokens_lo()
            with dve.Fori(0, turns) as item:
                c.enter(ITEM, item)

                def hidden(j):
                    c[s_msilu].step()
                    dve.wait_ge(s_msilu, c[s_msilu].now())
                    dve.wait_ge(s_mT, c[s_mT].now(1 if j >= 2 else 0))
                    nc.vector.tensor_tensor(m_h[:, j % 2], m_sg[:, j % 2], bank[j % 2][:, 256:512],
                                                              ALU.mult).then_inc(s_mread, c[s_mread].step())
                    c[s_mT].step()

                def hidden_lo(j):
                    k = slice(2 * j, 2 * j + 2)
                    c[s_mhi].step()
                    dve.wait_ge(s_mhi, c[s_mhi].now())
                    nc.vector.tensor_tensor(
                        m_lo[:, k].rearrange("p a s -> p (a s)"), bank[2 + j % 2][:, 0:256],
                        m_hi[:, k].rearrange("p a s -> p (a s)").bitcast(F32), ALU.subtract).then_inc(s_mlo, c[s_mlo].step())

                for j in range(GU_CHUNKS):
                    lo()
                    lo()
                    if j >= 1:
                        hidden(j - 1)
                    if j >= 2:
                        hidden_lo(j - 2)
                    if j == 2:
                        add_expert(0)
                    if j == 3:
                        add_expert(1)
                    if j == 4:
                        dve.wait_ge(s_putT, c[s_putT].now())
                        for t in range(TT):
                            ins = nc.vector.tensor_scalar(pick_w[:, t], slot_no[:, :], slot_of[:, t, bass.ds(item, 1)],
                                                          gate_of[:, t, bass.ds(item, 1)], ALU.is_equal, ALU.mult)
                        ins.then_inc(s_pickw, c[s_pickw].step())
                        c[s_putT].step()
                for kg in range(DOWN_GROUPS):
                    lo()
                    lo()
                    if kg == 0:
                        hidden(GU_CHUNKS - 1)
                        hidden_lo(GU_CHUNKS - 2)
                    if kg == 1:
                        hidden_lo(GU_CHUNKS - 1)
                    if kg == 2:
                        pick_tokens(item + 1)
                        c[s_xg].step(2)
                    if kg == 4:
                        tokens_lo()
                c.leave(ITEM, turns, {s_hi, s_split, s_pick, s_xg, s_ghi, s_glo, s_msilu, s_mT, s_mread, s_mhi, s_mlo,
                                      s_scat, s_added, s_putT, s_pickw})
            add_expert(0)
            add_expert(1)
            norm()

        @block.tensor
        def _(pe):
            slabs, c = Slabs(), counts_of()
            split = Count(s_split, RAW)

            def matmul(*a, **k):
                return nc.tensor.matmul(*a, **k)

            def next_slab():
                _, b = slabs.next()
                c[s_split].step()
                pe.wait_ge(s_split, c[s_split].now())
                return b

            def three(dst, left, right, start, stop):
                (lh, ll), (rh, rl) = left, right
                matmul(dst, lh, rh, start=start, stop=False)
                matmul(dst, ll, rh, start=False, stop=False)
                return matmul(dst, lh, rl, start=False, stop=stop)

            def wait_tile(k):
                if k % 2 == 0 and new_x[0]:
                    c[s_xlo].step()
                    pe.wait_ge(s_xlo, c[s_xlo].now())
                    new_x[0] -= 1

            new_x = [0]

            def unit(dst, features):
                b = next_slab()
                hi_, lo_ = (w[:, b].rearrange("p k (a n) -> p (k a) n", a=2) for w in (w_hi, w_lo))
                two = {"skip_group_check": True}
                for k in range(KT):
                    wait_tile(k)
                    for a in range(2):
                        out_ = dst[:, a * T:(a + 1) * T]
                        cols = slice(a * P, (a + 1) * P)
                        first, last = k == 0 and a == 0, k == KT - 1
                        if features:
                            (sh, sl), (mh, ml) = (hi_[:, k, cols], lo_[:, k, cols]), (x_hi[:, k], x_lo[:, k])
                        else:
                            (sh, sl), (mh, ml) = (x_hi[:, k, cols], x_lo[:, k, cols]), (hi_[:, k], lo_[:, k])
                        matmul(out_, sh, mh, start=first, stop=False, **two)
                        matmul(out_, sl, mh, start=False, stop=False, **two)
                        ins = matmul(out_, sh, ml, start=False, stop=last, **two)
                ins.then_inc(s_free, c[s_free].step())

            def out_slab(ch, kh, xh, xl):
                b = next_slab()
                for kl in range(SK):
                    k = kh * SK + kl
                    for t in range(TT):
                        tok = slice(t * P, (t + 1) * P)
                        ins = three(bank[3 * ch + t][:, :], (xh[:, k, tok], xl[:, k, tok]),
                                    (w_hi[:, b, kl], w_lo[:, b, kl]), start=k == 0, stop=k == KT - 1)
                ins.then_inc(s_free, c[s_free].step())

            def by_features(banks):
                for kh in range(2):
                    b = next_slab()
                    for kl in range(SK):
                        k = kh * SK + kl
                        wait_tile(k)
                        for blk in range(4):
                            f = slice(blk * P, (blk + 1) * P)
                            dst = banks[blk // 2][:, (blk % 2) * T:(blk % 2 + 1) * T]
                            first, last = k == 0 and blk % 2 == 0, k == KT - 1
                            two = {"skip_group_check": True}
                            matmul(dst, w_hi[:, b, kl, f], x_hi[:, k], start=first, stop=False, **two)
                            matmul(dst, w_hi[:, b, kl, f], x_lo[:, k], start=False, stop=False, **two)
                            ins = matmul(dst, w_lo[:, b, kl, f], x_hi[:, k], start=False, stop=last, **two)
                    ins.then_inc(s_free, c[s_free].step())

            def transpose_pair(b, dst, cols):
                for kk in range(2):
                    for t in range(TT):
                        ins = nc.tensor.transpose(dst[:, kk * T + t * P:kk * T + (t + 1) * P],
                                                  hn[:, t, cols(2 * b + kk)], ident[:, :])
                ins.then_inc(s_xT, c[s_xT].step())

            def transpose_x(cols):
                for b in range(4):
                    if b % 2 == 0:
                        c[s_hn].step()
                        pe.wait_ge(s_hn, c[s_hn].now())
                    transpose_pair(b, bank[b], cols)
                new_x[0] = 4

            nc.tensor.sem_inc(s_free, SPLIT)
            pe.wait_ge(s_const, 2)
            transpose_x(plain_tile)

            tiles = ((slice(0, P), slice(0, P)), (slice(P, T), slice(0, P)), (slice(P, T), slice(P, T)))

            def qk_part(tile, n, g, tok):
                q, i = divmod(n, QH)
                rows = slice((i % 2) * DH, (i % 2 + 1) * DH)
                return tile[rows, q % 2, g, (i // 2) * T + tok.start:(i // 2) * T + tok.stop]

            def scores(n):
                for g in range(G):
                    if n >= 1:
                        pe.wait_ge(s_scread, (n - 1) * G + g + 1)
                    matmul(bank[2 + g][:, 0:P], qk_part(a_qT, n, g, slice(0, P)), qk_part(a_kT, n, g, slice(0, P)),
                           start=True, stop=True)
                    matmul(bank[2 + g][:, P:SEEN], qk_part(a_qT, n, g, slice(P, T)), qk_part(a_kT, n, g, slice(0, T)),
                           start=True, stop=True).then_inc(s_scores, 1)

            def transpose_p(n, g):
                m = n * G + g
                if g == 0:
                    pe.wait_ge(s_exp, n + 1)
                if m >= 2:
                    pe.wait_ge(s_pTread, m - 1)
                for a in range(3):
                    ins = nc.tensor.transpose(bank[5 + m % 2][:, a * P:(a + 1) * P],
                                              a_s[:, n % 2, g, a * P:(a + 1) * P], ident[:, :])
                ins.then_inc(s_pT, 1)

            def weigh_v(n, g):
                m, (q, i) = n * G + g, divmod(n, QH)
                pe.wait_ge(s_pTread, m + 1)
                if g == 0 and n >= 1:
                    pe.wait_ge(s_y, n)
                for a, (qt, kt) in enumerate(((0, 0), (1, 0), (1, 1))):
                    v = a_v[:, q % 2, g, kt * QN + i * DH:kt * QN + (i + 1) * DH]
                    ins = matmul(bank[7][:, qt * DH:(qt + 1) * DH], a_pT[:, m % 2, a * P:(a + 1) * P], v,
                                 start=g == 0 and a == 0, stop=g == G - 1 and a in (0, 2), skip_group_check=True)
                ins.then_inc(s_pv, 1)

            for q in range(QUARTERS + 1):
                for u in range(DIL_UNITS):
                    if q < QUARTERS:
                        if q * DIL_UNITS + u >= 2:
                            c[s_qkv].step()
                            pe.wait_ge(s_qkv, c[s_qkv].now())
                        unit(bank[(q * DIL_UNITS + u) % 2], u % 3 < 2)
                    if q == 0:
                        continue
                    n = (q - 1) * QH + u // 2
                    if u == 0:
                        pe.wait_ge(s_qkv, q * DIL_UNITS)
                        scores(n)
                        if q == QUARTERS:
                            pe.wait_ge(s_y, 2 * QH)
                            transpose_pair(0, bank[0], plain_tile)
                            transpose_pair(1, bank[1], plain_tile)
                    elif u % 2 == 1:
                        transpose_p(n, 0)
                        transpose_p(n, 1)
                        if u // 2 < QH - 1:
                            scores(n + 1)
                        weigh_v(n, 0)
                        transpose_p(n, 2)
                        weigh_v(n, 1)
                    else:
                        weigh_v(n - 1, 2)
                        if q == QUARTERS and u == 2:
                            pe.wait_ge(s_y, 3 * QH)
                            pe.wait_ge(s_xlo, 5)
                            transpose_pair(2, bank[0], plain_tile)
                        if q == QUARTERS and u == 4:
                            pe.wait_ge(s_xlo, 7)
                            out_slab(0, 0, x_hi, x_lo)
            pe.wait_ge(s_y, H)
            transpose_pair(3, bank[2], plain_tile)
            c[s_xlo].step(4)
            pe.wait_ge(s_xlo, c[s_xlo].now())
            out_slab(0, 1, x_hi, x_lo)
            out_slab(1, 0, x_hi, x_lo)
            out_slab(1, 1, x_hi, x_lo)

            pe.wait_ge(s_h, 2)
            transpose_x(adjacent_tile)
            for j in range(GU_CHUNKS):
                if j >= 2:
                    pe.wait_ge(s_gu, j - 1)
                by_features([bank[4 + 2 * (j % 2) + n] for n in range(2)])
            pe.wait_ge(s_gu, GU_CHUNKS)
            for kg in range(DOWN_GROUPS):
                pe.wait_ge(s_flo, 2 * kg + 2)
                for half in range(2):
                    b = next_slab()
                    for kl in range(SK):
                        k = kg * SK + kl
                        for t in range(TT):
                            tok = slice(t * P, (t + 1) * P)
                            ins = three(bank[2 * t + half][:, :], (f_hi[:, k, tok], f_lo[:, k, tok]),
                                        (w_hi[:, b, kl], w_lo[:, b, kl]), start=k == 0, stop=k == FF // P - 1)
                    ins.then_inc(s_free, c[s_free].step())

            pe.wait_ge(s_h, 3)
            transpose_x(plain_tile)

            def head_part(tile, n, tok):
                return tile[(n % 2) * DH:(n % 2 + 1) * DH, n // 2, tok]

            def head_slot(n):
                if n < H:
                    if n >= 2:
                        pe.wait_ge(s_zread, n - 1)
                    z = bank[2 + n % 2]
                    matmul(z[:, 0:T], head_part(b_kT, n, slice(0, P)), head_part(b_qT, n, slice(0, T)), start=True,
                           stop=True)
                    matmul(z[:, T:SEEN], head_part(b_kT, n, slice(P, T)), head_part(b_qT, n, slice(P, T)), start=True,
                           stop=True).then_inc(s_z, 1)
                if 0 <= n - 1 < H:
                    m = n - 1
                    pe.wait_ge(s_spm, m + 1)
                    if m >= 2:
                        pe.wait_ge(s_arg, m - 1)
                    sums = bank[4 + m % 2]
                    matmul(sums[:, 0:SEEN], from_on[:, :], b_sp[:, m % 2], start=True, stop=False)
                    matmul(sums[:, P:T], ones[:, :], b_sp[:, m % 2, T:SEEN], start=False, stop=True).then_inc(s_cum, 1)
                if n - 2 >= 0:
                    m = n - 2
                    pe.wait_ge(s_att, m + 1)
                    if m >= 4 and m % 2 == 0:
                        pe.wait_ge(s_olo, m // 2 - 1)
                    q, i = divmod(m, QH)
                    rows = slice((m % 2) * DH, (m % 2 + 1) * DH)
                    o = bank[6 + m // 2 % 2]
                    for kt in range(2):
                        v = b_v[:, q, kt * QN + i * DH:kt * QN + (i + 1) * DH]
                        ins = matmul(o[rows, kt * P:T], v, b_att[:, m % 2, kt * T:T + kt * P], start=kt == 0,
                                     stop=kt == 1)
                    ins.then_inc(s_o, 1)

            read = QUARTERS * DIL_UNITS
            for q in range(QUARTERS):
                for u in range(SB_UNITS):
                    m = q * SB_UNITS + u
                    if m >= 2:
                        pe.wait_ge(s_qkv, read + m - 1)
                    unit(bank[m % 2], u < 2)
                    if m in HEADS_AFTER:
                        pe.wait_ge(s_qkv, read + q * SB_UNITS)
                    for n in HEADS_AFTER.get(m, []):
                        head_slot(n)
            pe.wait_ge(s_qkv, read + QUARTERS * SB_UNITS)
            head_slot(12)
            pe.wait_ge(s_olo, 4)
            out_slab(0, 0, y_hi, y_lo)
            for n in range(13, H + 2):
                head_slot(n)
            pe.wait_ge(s_olo, H // 2)
            out_slab(0, 1, y_hi, y_lo)
            out_slab(1, 0, y_hi, y_lo)
            out_slab(1, 1, y_hi, y_lo)

            pe.wait_ge(s_h, 5)
            transpose_x(adjacent_tile)
            new_x[0] = 0
            c[s_xlo].step(4)
            pe.wait_ge(s_xlo, c[s_xlo].now())
            pe.wait_ge(s_wrt, 16)
            for t in range(TT):
                tok = slice(t * P, (t + 1) * P)
                for k in range(KT):
                    for part, xx in enumerate((x_hi, x_lo)):
                        ins = matmul(bank[4][:, t * NE:(t + 1) * NE], xx[:, k, tok].bitcast(F32), w_rt[:, k],
                                     start=k == 0 and part == 0, stop=k == KT - 1 and part == 1)
            ins.then_inc(s_lg, 1)
            pe.wait_ge(s_took, 1)
            took = r["took"]
            matmul(bank[5][:, 0:NE], before[:, :], took[:, 0], start=True, stop=True)
            matmul(bank[5][:, NE:2 * NE], ones[:, :], took[:, 0], start=True, stop=False)
            matmul(bank[5][:, NE:2 * NE], before[:, :], took[:, 1], start=False, stop=True)
            matmul(bank[5][:, 2 * NE:3 * NE], ones[:, :], took[:, 0], start=True, stop=False)
            matmul(bank[5][:, 2 * NE:3 * NE], ones[:, :], took[:, 1], start=False, stop=True).then_inc(s_rank, 1)
            pe.wait_ge(s_routed, 1)
            turns = pe.value_load(turns_i[0:1, 0:1], min_val=NE, max_val=2 * NE)

            def gather():
                c[s_pick].step()
                pe.wait_ge(s_pick, c[s_pick].now())
                for b in range(2):
                    for kk in range(4):
                        k = 4 * b + kk
                        for t in range(TT):
                            ins = matmul(bank[6 + b][:, kk * P:(kk + 1) * P], hn[:, t, adjacent_tile(k)], pick[:, t],
                                         start=t == 0, stop=t == TT - 1)
                    ins.then_inc(s_xg, c[s_xg].step())

            def scatter(t):
                if t == 0:
                    pe.wait_ge(s_yread, c[s_yread].now())
                for n in range(2):
                    pe.wait_ge(s_added, c[s_added].now())
                    matmul(bank[6 + n][:, :], put_w[:, t * P:(t + 1) * P],
                                            yg[:, n * SN:(n + 1) * SN], start=True, stop=True).then_inc(s_scat, c[s_scat].step())
                c[s_added].step(2)

            gather()
            with pe.Fori(0, turns) as item:
                c.enter(ITEM, item)

                def transpose_hidden(j):
                    c[s_mread].step()
                    pe.wait_ge(s_mread, c[s_mread].now())
                    pe.wait_ge(s_mlo, c[s_mlo].now(1 if j >= 2 else 0))
                    for a in range(2):
                        ins = nc.tensor.transpose(bank[2 + j % 2][:, a * P:(a + 1) * P],
                                                  m_h[:, j % 2, a * P:(a + 1) * P], ident[:, :])
                    ins.then_inc(s_mT, c[s_mT].step())
                    c[s_mlo].step()

                c[s_glo].step(2)
                pe.wait_ge(s_glo, c[s_glo].now())
                for j in range(GU_CHUNKS):
                    for kh in range(2):
                        b = next_slab()
                        for kl in range(SK):
                            k = kh * SK + kl
                            ins = three(bank[j % 2][:, :], (g_hi[:, k], g_lo[:, k]), (w_hi[:, b, kl], w_lo[:, b, kl]),
                                        start=k == 0, stop=k == KT - 1)
                        ins.then_inc(s_free, c[s_free].step())
                    if j >= 1:
                        transpose_hidden(j - 1)
                    if j == 1:
                        scatter(0)
                    if j == 2:
                        scatter(1)
                    if j == 4:
                        c[s_pickw].step()
                        pe.wait_ge(s_pickw, c[s_pickw].now())
                        pe.wait_ge(s_added, c[s_added].now())
                        for t in range(TT):
                            ins = nc.tensor.transpose(bank[6][:, t * P:(t + 1) * P], pick_w[:, t], ident[:, :])
                        ins.then_inc(s_putT, c[s_putT].step())
                for kg in range(DOWN_GROUPS):
                    if kg == 1:
                        transpose_hidden(GU_CHUNKS - 1)
                    if kg == 0:
                        pe.wait_ge(s_mlo, c[s_mlo].now(GU_CHUNKS - 3))
                        pe.wait_ge(s_yread, c[s_yread].now())
                    else:
                        pe.wait_ge(s_mlo, c[s_mlo].now(GU_CHUNKS - 2 * kg - 2))
                    for half in range(2):
                        b = next_slab()
                        for kl in range(SK):
                            k = kg * SK + kl
                            ins = three(bank[4 + half][:, :], (m_hi[:, k], m_lo[:, k]),
                                        (w_hi[:, b, kl], w_lo[:, b, kl]), start=k == 0, stop=k == FF // P - 1)
                        ins.then_inc(s_free, c[s_free].step())
                    if kg == 3:
                        c[s_put].step()
                        pe.wait_ge(s_put, c[s_put].now())
                        gather()
                c[s_yread].step()
                c.leave(ITEM, turns, {s_split, s_free, s_glo, s_mread, s_mlo, s_mT, s_scat, s_added, s_pickw,
                                      s_putT, s_put, s_pick, s_xg, s_yread})
            scatter(0)
            scatter(1)


_INS = ["x", "mix_norm", "ffn_norm", "dil_w_in", "dil_w_out", "sb_w_qkv", "sb_w_out", "ffn_w_gate_up", "ffn_w_down",
        "moe_w_router", "moe_w_gate_up", "moe_w_down", "final_norm"]


def kernel(**inputs):
    import concourse.bacc as bacc
    from concourse.bass_utils import run_bass_kernel_spmd

    nc = bacc.Bacc("TRN2", target_bir_lowering=False, num_devices=1)
    arrays, args = {}, []
    for name in _INS:
        a = np.ascontiguousarray(inputs[name])
        arrays[f"in_{name}"] = a
        args.append(nc.dram_tensor(f"in_{name}", a.shape, mybir.dt.from_np(a.dtype), kind="ExternalInput").ap())
    out = nc.dram_tensor("out", (1, T, D), F32, kind="ExternalOutput").ap()
    trunk(nc, *args, out)
    res = run_bass_kernel_spmd(nc, [arrays], core_ids=[0])
    return res.results[0]["out"]
```

```python
import numpy as np
import concourse.bass as bass
from concourse import mybir
from concourse.alu_op_type import AluOpType as ALU
from contextlib import ExitStack

F32 = mybir.dt.float32
F32R = mybir.dt.float32r
I32 = mybir.dt.int32
ACT = mybir.ActivationFunctionType
AX = mybir.AxisListType

P = 128
T = 256
TT = T // P
D = 1024
KT = D // P
H, DH = 16, 64
G = 3
FF = 3584
NE = 8
QUARTERS, QH = 4, 4
QN = QH * DH
SEEN = 3 * P
ROOT_D_BITS = (D.bit_length() - 1) // 2
assert D == 4 ** ROOT_D_BITS
EPS = 1e-6
MASKED = 1e30

SK, SN = 4, 512
RAW, SPLIT = 7, 3
GU_CHUNKS = FF // 256
DOWN_GROUPS = FF // (SK * P)
DIL_UNITS = 3 * G
SB_UNITS = 3
OUT_SLABS = 4
FFN_SLABS = 2 * GU_CHUNKS + 2 * DOWN_GROUPS
DENSE_SLABS = QUARTERS * (DIL_UNITS + SB_UNITS) + 2 * OUT_SLABS + FFN_SLABS


def adjacent_tile(k):
    return slice((k // SK) * SK * P + k % SK, (k // SK + 1) * SK * P, SK)


def plain_tile(k):
    return slice(k * P, (k + 1) * P)


HEADS_IN = {3: ([0], [1]), 4: ([], [2]), 5: ([3], []), 6: ([4], [5]), 7: ([], [6]), 8: ([7], []),
            9: ([8], [9]), 10: ([], [10]), 11: ([11], [])}


class Count:

    def __init__(self, sem, start=0):
        self.sem, self.n, self.turn, self.per = sem, start, None, 0

    def step(self, by=1):
        self.n += by
        return by

    def enter(self, turn, per):
        assert self.turn is None
        self.turn, self.per, self.first = turn, per, self.n

    def leave(self, turns):
        assert self.n - self.first == self.per, (self.sem, self.n - self.first, self.per)
        if isinstance(turns, int):
            self.turn, self.n = None, self.first + turns * self.per
        else:
            self.turn, self.n = turns, self.first

    def now(self, back=0):
        v = self.n - back
        return v if self.turn is None else self.turn * self.per + v


class Slabs:

    def __init__(self):
        self.s = 0

    def next(self):
        s, self.s = self.s, self.s + 1
        return s % RAW, s % SPLIT


def trunk(nc, x, mix_norm, ffn_norm, dil_w_in, dil_w_out, sb_w_qkv, sb_w_out, ffn_w_gate_up, ffn_w_down,
          moe_w_router, moe_w_gate_up, moe_w_down, final_norm, out):
    ctx = ExitStack()
    with ctx:
        at = [nc.sbuf_base + (-nc.sbuf_base) % 64]

        def place(name, shape, dt=F32, offset=None):
            size = int(np.prod(shape[1:])) * 4
            if offset is None:
                offset, at[0] = at[0], at[0] + size + (-size) % 64
            return nc.alloc_sbuf_tensor_at(name, shape, dt, offset=offset)

        raw = place("raw", [P, RAW, SK, SN])
        w_hi = place("w_hi", [P, SPLIT, SK, SN], F32R)
        w_lo = place("w_lo", [P, SPLIT, SK, SN], F32R)
        h = place("h", [P, TT, D])
        hn = place("hn", [P, TT, D])
        x_hi = place("x_hi", [P, KT, T], F32R)
        x_lo = place("x_lo", [P, KT, T], F32R)
        gains = place("gains", [P, D])
        ident = place("ident", [P, P])
        ones = place("ones", [P, P])
        before = place("before", [P, P])
        from_on = place("from_on", [P, P])
        slot_no = place("slot_no", [P, P])
        negslope = place("negslope", [P, H])
        ssq = place("ssq", [P, 2, TT])
        rstd = place("rstd", [P, TT])
        total = place("total", [P, TT])
        mean = place("mean", [P, TT])
        guess = place("guess", [P, TT], I32)
        newton = place("newton", [P, TT])
        region = at[0]

        a_qT = place("a_qT", [P, 2, G, 2 * T])
        a_kT = place("a_kT", [P, 2, G, 2 * T])
        a_v = place("a_v", [P, 2, G, TT * QN])
        a_s = place("a_s", [P, 2, G, SEEN])
        a_pT = place("a_pT", [P, 2, SEEN])
        dist = place("dist", [P, G, SEEN])
        d_int = place("d_int", [P, SEEN], I32)
        nmax = place("nmax", [P, 2, TT])
        zsum = place("zsum", [P, 2, TT])
        zinv = place("zinv", [P, TT])
        d_hi = place("d_hi", [P, SK, T], F32R)
        d_lo = place("d_lo", [P, SK, T], F32R)
        ends = [at[0]]

        at[0] = region
        f_hi = place("f_hi", [P, FF // P, T], F32R)
        f_lo = place("f_lo", [P, FF // P, T], F32R)
        f_sg = place("f_sg", [P, 2, 512])
        f_h = place("f_h", [P, 2, 512])
        ends.append(at[0])

        at[0] = region
        b_qT = place("b_qT", [P, H // 2, T])
        b_kT = place("b_kT", [P, H // 2, T])
        b_v = place("b_v", [P, QUARTERS, TT * QN])
        y_hi = place("y_hi", [P, KT, T], F32R)
        y_lo = place("y_lo", [P, KT, T], F32R)
        b_l = place("b_l", [P, 2, 3 * P])
        b_sp = place("b_sp", [P, 2, 3 * P])
        b_z = place("b_z", [P, 2, 3 * P])
        b_att = place("b_att", [P, 2, 3 * P])
        keep = place("keep", [P, 3 * P])
        hide = place("hide", [P, 3 * P])
        ends.append(at[0])

        at[0] = region
        m_hi = place("m_hi", [P, FF // P, P], F32R)
        m_lo = place("m_lo", [P, FF // P, P], F32R)
        g_hi = place("g_hi", [P, KT, P], F32R)
        g_lo = place("g_lo", [P, KT, P], F32R)
        m_sg = place("m_sg", [P, 2, 256])
        m_h = place("m_h", [P, 2, 256])
        out_hi = place("out_hi", [P, D], F32R)
        out_lo = place("out_lo", [P, D], F32R)
        pick = place("pick", [P, TT, P])
        put = place("put", [P, TT * P], F32R)
        gate_now = place("gate_now", [P, TT])
        slot_gate = place("slot_gate", [P, 1])
        w_rt = place("w_rt", [P, KT, NE])
        w_rt2 = place("w_rt2", [P, KT, 2, NE], F32R)
        lgT = place("lgT", [2 * NE, T])
        fold = place("fold", [2 * NE, NE])
        names = ["cand", "one1", "one2", "lg2", "took", "gate", "tmp", "rev", "rank"]
        r = {n: place("r_" + n, [P, TT, NE]) for n in names}
        small = {n: place("r_" + n, [P, TT]) for n in ["m1", "c1", "m2", "c2", "d", "e", "den", "w1", "w2"]}
        slot_of = place("slot_of", [P, TT, 2 * NE + 1])
        gate_of = place("gate_of", [P, TT, 2 * NE + 1])
        counts = place("counts", [P, NE])
        most = place("most", [P, 1])
        turns_f = place("turns_f", [P, 1])
        turns_i = place("turns_i", [P, 1], I32)
        ends.append(at[0])
        assert max(ends) <= nc.sbuf_usable_end, (ends, nc.sbuf_usable_end)

        bank = [ctx.enter_context(nc.psum_tensor(f"bank{b}", [P, 512], F32)) for b in range(8)]

        def sem(name):
            return ctx.enter_context(nc.semaphore(name))

        raw_full = [sem(f"raw_full{i}") for i in range(RAW)]
        s_hi = sem("hi_made")
        s_split = sem("split_made")
        s_free = sem("split_free")
        s_x = [sem(f"x_loaded{t}") for t in range(TT)]
        s_gain = sem("gain_loaded")
        s_const = sem("const_made")
        s_dint = sem("dint_used")
        s_dmask = sem("dmask_made")
        s_ssq = sem("ssq_made")
        s_nstep = sem("norm_step")
        s_hn = sem("hn_made")
        s_xT = sem("xT_made")
        s_xhi = sem("xhi_made")
        s_xlo = sem("xlo_made")
        s_qkv = sem("qkv_read")
        s_first = sem("first_tile_made")
        s_h = sem("h_made")
        s_scores = sem("scores_made")
        s_scread = sem("scores_read")
        s_max = sem("max_made")
        s_exp = sem("exp_made")
        s_pT = sem("pT_made")
        s_pTread = sem("pT_read")
        s_pv = sem("pv_made")
        s_zinv = sem("zinv_made")
        s_y = sem("y_made")
        s_silu = sem("silu_made")
        s_gu = sem("gu_read")
        s_fhi = sem("f_hi_made")
        s_flo = sem("f_lo_made")
        s_z = sem("z_made")
        s_zread = sem("z_read")
        s_astep = sem("act_step")
        s_sp = sem("sp_made")
        s_spm = sem("sp_masked")
        s_cum = sem("cum_made")
        s_arg = sem("arg_made")
        s_att = sem("att_made")
        s_o = sem("o_made")
        s_ohi = sem("o_hi_made")
        s_olo = sem("o_lo_made")
        s_wrt = sem("router_loaded")
        s_rthi = sem("router_hi_made")
        s_rtlo = sem("router_lo_made")
        s_lgT = sem("logitsT_made")
        s_lgTread = sem("logitsT_read")
        s_lg = sem("logits_made")
        s_rstep = sem("route_step")
        s_took = sem("took_made")
        s_diff = sem("logit_diff_made")
        s_e2 = sem("gate_exp_made")
        s_rank = sem("rank_made")
        s_routed = sem("routed")
        s_clear = sem("cleared")
        s_pick = sem("pick_made")
        s_xg = sem("gathered")
        s_ghi = sem("g_hi_made")
        s_glo = sem("g_lo_made")
        s_msilu = sem("expert_silu_made")
        s_mread = sem("expert_gu_read")
        s_mT = sem("expert_hT_made")
        s_mhi = sem("m_hi_made")
        s_mlo = sem("m_lo_made")
        s_outhi = sem("expert_out_hi_made")
        s_outlo = [sem(f"expert_out_lo_made{half}") for half in range(2)]
        s_gate = sem("gate_now_made")
        s_putT = sem("put_made")
        s_put = sem("put_read")
        s_scat = sem("scattered")
        s_added = sem("added")
        s_out = sem("out_stored")

        ITEM = {s_hi: FFN_SLABS, s_split: FFN_SLABS, s_free: FFN_SLABS, s_pick: 1, s_xg: 2, s_ghi: 2, s_glo: 2,
                s_msilu: GU_CHUNKS, s_mread: GU_CHUNKS, s_mT: GU_CHUNKS, s_mhi: GU_CHUNKS,
                s_mlo: GU_CHUNKS, s_outhi: 2, s_outlo[0]: 1, s_outlo[1]: 1,
                s_gate: 1, s_putT: 1, s_put: 1, s_scat: 4, s_added: 4}

        def counts_of():
            class Counts(dict):
                def __missing__(self, s):
                    self[s] = Count(s, {s_split: RAW, s_free: SPLIT}.get(s, 0))
                    return self[s]

                def enter(self, per, turn):
                    for s, n in per.items():
                        self[s].enter(turn, n)

                def leave(self, per, turns, used):
                    for s, n in per.items():
                        if s not in used:
                            self[s].n = self[s].first + n
                        self[s].leave(turns)
            return Counts()

        block = ctx.enter_context(nc.Block())

        @block.sync
        def _(sp):
            slabs = Slabs()
            free = Count(s_split)

            def load(src, narrow=False):
                slot, _ = slabs.next()
                free.step()
                sp.wait_ge(s_split, free.now())
                dst = raw[:, slot].rearrange("p k (a n) -> p (k a) n", a=2) if narrow else raw[:, slot]
                sp.dma_start(dst, src).then_inc(raw_full[slot], 16)

            def square(w, kh, cols):
                return w[kh * SK * P:(kh + 1) * SK * P, cols].rearrange("(k p) n -> p k n", p=P)

            def load_out(w):
                for kh in range(2):
                    for ch in range(2):
                        load(square(w, kh, slice(ch * SN, (ch + 1) * SN)))

            def load_unit(w, col):
                load(w[:, col:col + QN].rearrange("(k p) n -> p k n", p=P), True)

            def load_gate_up(w):
                for j in range(GU_CHUNKS):
                    for kh in range(2):
                        v = w[kh * SK * P:(kh + 1) * SK * P, :]
                        v = v.rearrange("(p k) (a f) -> p (k a) f", p=P, a=2)
                        load(v[:, :, j * 256:(j + 1) * 256], True)

            def load_down(w):
                for kg in range(DOWN_GROUPS):
                    for half in range(2):
                        load(square(w, kg, slice(half * SN, (half + 1) * SN)))

            for t in range(TT):
                sp.dma_start(h[:, t], x[0, t * P:(t + 1) * P]).then_inc(s_x[t], 16)
            for q in range(QUARTERS):
                for u in range(DIL_UNITS):
                    load_unit(dil_w_in[0], u * D + q * QN)
            load_out(dil_w_out[0])
            load_gate_up(ffn_w_gate_up[0])
            load_down(ffn_w_down[0])
            for q in range(QUARTERS):
                for u in range(SB_UNITS):
                    load_unit(sb_w_qkv[0], u * D + q * QN)
            load_out(sb_w_out[0])

            def load_expert(e):
                load_gate_up(moe_w_gate_up[0, bass.ds(e, 1)].squeeze(0))
                load_down(moe_w_down[0, bass.ds(e, 1)].squeeze(0))

            with sp.Fori(0, NE) as e:
                free.enter(e, FFN_SLABS)
                load_expert(e)
                free.leave(NE)
            sp.wait_ge(s_routed, 1)
            turns = sp.value_load(turns_i[0:1, 0:1], min_val=NE, max_val=2 * NE)
            with sp.If(turns > NE):
                with sp.Fori(0, NE) as e:
                    free.enter(e, FFN_SLABS)
                    load_expert(e)
                    free.leave(NE)
            with sp.Else():
                pass
            for n in range(2):
                slot, _ = slabs.next()
                sp.wait_ge(s_split, turns * FFN_SLABS + DENSE_SLABS + n + 1)
                sp.sem_inc(raw_full[slot], 16)
            for half in range(2):
                cols = slice(half * SN, (half + 1) * SN)
                sp.wait_ge(s_hn, 4 * 4 + 2 * (half + 1))
                sp.dma_start(out[0, :, cols].rearrange("(t p) d -> p t d", p=P), hn[:, :, cols]).then_inc(s_out, 16)
            sp.wait_ge(s_out, 32)

        @block.gpsimd
        def _(pool):
            def gain(n, row):
                if n >= 1:
                    pool.wait_ge(s_hn, 4 * n)
                pool.dma_start(gains[:, :], row.partition_broadcast(P)).then_inc(s_gain, 16)

            gain(0, mix_norm[0])
            nc.gpsimd.memset(ones[:, :], 1.0)
            nc.gpsimd.memset(ident[:, :], 0.0)
            for hd in range(H):
                nc.gpsimd.memset(negslope[:, hd:hd + 1], -(2.0 ** (-8.0 * (hd + 1) / H)))
            nc.gpsimd.iota(slot_no[:, :], [[1, P]], base=0, channel_multiplier=0,
                           allow_small_or_imprecise_dtypes=True)
            for k0, n, base in ((0, P, 0), (P, T, P)):
                nc.gpsimd.iota(d_int[:, k0:k0 + n], [[-1, n]], base=base, channel_multiplier=1)
                ins = nc.gpsimd.iota(dist[:, 0, k0:k0 + n], [[-1, n]], base=base, channel_multiplier=1,
                                     allow_small_or_imprecise_dtypes=True)
            ins.then_inc(s_const, 1)
            pool.wait_ge(s_const, 1)
            nc.gpsimd.affine_select(out=ident[:, :], in_=ident[:, :], compare_op=ALU.not_equal, fill=1.0,
                                    base=0, pattern=[[-1, P]], channel_multiplier=1)
            nc.gpsimd.affine_select(out=before[:, :], in_=ones[:, :], compare_op=ALU.is_ge, fill=0.0,
                                    base=-1, pattern=[[1, P]], channel_multiplier=-1)
            nc.gpsimd.affine_select(out=from_on[:, :], in_=ones[:, :], compare_op=ALU.is_ge, fill=0.0,
                                    base=0, pattern=[[-1, P]], channel_multiplier=1).then_inc(s_const, 1)
            pool.wait_ge(s_dint, 6)
            for k0, n, base in ((0, P, 0), (P, T, P)):
                ins = nc.gpsimd.affine_select(out=dist[:, 0, k0:k0 + n], in_=dist[:, 0, k0:k0 + n],
                                              compare_op=ALU.is_ge, fill=MASKED, base=P - base, pattern=[[1, n]],
                                              channel_multiplier=-1)
            ins.then_inc(s_dmask, 1)
            pool.wait_ge(s_dmask, 1)
            for g in range(G):
                for k0, n, base in ((0, P, 0), (P, T, P)):
                    ins = nc.gpsimd.affine_select(out=dist[:, g, k0:k0 + n], in_=dist[:, g, k0:k0 + n],
                                                  compare_op=ALU.is_ge, fill=MASKED, base=base, pattern=[[-1, n]],
                                                  channel_multiplier=1)
            ins.then_inc(s_dmask, 1)
            gain(1, ffn_norm[0])
            for j in range(GU_CHUNKS):
                pool.wait_ge(s_fhi, j + 1)
                nc.gpsimd.tensor_tensor(f_lo[:, 2 * j:2 * j + 2].rearrange("p a t -> p (a t)"), f_h[:, j % 2],
                                        f_hi[:, 2 * j:2 * j + 2].rearrange("p a t -> p (a t)").bitcast(F32),
                                        ALU.subtract).then_inc(s_flo, 1)
                if j == 0:
                    gain(2, mix_norm[1])
            pool.wait_ge(s_h, 8)
            nc.gpsimd.memset(keep[:, :], 1.0)
            nc.gpsimd.memset(hide[:, :], 0.0).then_inc(s_const, 1)
            pool.wait_ge(s_const, 3)
            for c0, n in ((0, T), (T, P)):
                for m, fill in ((keep, 0.0), (hide, -MASKED)):
                    nc.gpsimd.affine_select(out=m[:, c0:c0 + n], in_=m[:, c0:c0 + n], compare_op=ALU.is_ge,
                                            fill=fill, base=-1, pattern=[[1, n]],
                                            channel_multiplier=-1).then_inc(s_const, 1)
            pool.wait_ge(s_const, 7)
            for i in range(H):
                pool.wait_ge(s_sp, i + 1)
                nc.gpsimd.tensor_tensor(b_sp[:, i % 2], b_sp[:, i % 2], keep[:, :], ALU.mult).then_inc(s_spm, 1)
                if i == 0:
                    gain(3, ffn_norm[1])
            pool.wait_ge(s_h, 12)
            pool.dma_start(w_rt[:, :, :].rearrange("p (a k) e -> p a k e", a=2),
                           moe_w_router[0].rearrange("(a p k) e -> p a k e", p=P, k=SK)).then_inc(s_wrt, 16)
            nc.gpsimd.memset(out_hi[:, :].bitcast(F32), 0.0)
            nc.gpsimd.memset(out_lo[:, :].bitcast(F32), 0.0)
            nc.gpsimd.memset(slot_of[:, :, :], -1.0)
            nc.gpsimd.memset(gate_of[:, :, :], 0.0)
            nc.gpsimd.iota(r["rev"][:, :, :], [[0, TT], [-1, NE]], base=NE, channel_multiplier=0,
                           allow_small_or_imprecise_dtypes=True)
            nc.gpsimd.tensor_tensor(fold[:, :], ident[0:2 * NE, 0:NE], ident[0:2 * NE, NE:2 * NE], ALU.add)
            nc.gpsimd.memset(put[:, :].bitcast(F32), 0.0).then_inc(s_clear, 1)
            gain(4, final_norm)

        @block.scalar
        def _(act):
            slabs, c = Slabs(), counts_of()
            filled = [Count(s) for s in raw_full]
            done = Count(s_free, SPLIT)

            def hi():
                a, b = slabs.next()
                filled[a].step(16)
                act.wait_ge(raw_full[a], filled[a].now())
                c[s_free].step()
                act.wait_ge(s_free, c[s_free].now())
                nc.scalar.activation(w_hi[:, b], raw[:, a], ACT.Copy).then_inc(s_hi, c[s_hi].step())

            c[s_free].n = 0

            def sum_squares(half, t):
                cols = slice(half * SN, (half + 1) * SN)
                return nc.scalar.activation(hn[:, t, cols], h[:, t, cols], ACT.Square,
                                            accum_out=ssq[:, half, t:t + 1])

            def norm(n):
                for half in range(2):
                    for t in range(TT):
                        act.wait_ge(s_h, (n - 1) * 2 * TT + half * TT + t + 1)
                        ins = sum_squares(half, t)
                ins.then_inc(s_ssq, 1)

            def x_hi_parts():
                for b in range(4):
                    c[s_xT].step()
                    act.wait_ge(s_xT, c[s_xT].now())
                    nc.scalar.activation(
                        x_hi[:, 2 * b:2 * b + 2].rearrange("p k t -> p (k t)"), bank[b][:, :],
                        ACT.Copy).then_inc(s_xhi, c[s_xhi].step())

            def ahead():
                hi()

            def y_hi_parts():
                c[s_xT].step()
                b = (c[s_xT].n - 1) % 4
                dst = (d_hi[:, 2 * b:2 * b + 2] if b < 2 else x_hi[:, 2 * b:2 * b + 2]).rearrange("p k t -> p (k t)")
                act.wait_ge(s_xT, c[s_xT].now())
                nc.scalar.activation(dst, bank[(4, 6, 4, 2)[b]][:, :], ACT.Copy).then_inc(s_xhi, c[s_xhi].step())

            for t in range(TT):
                act.wait_ge(s_x[t], 16)
                for half in range(2):
                    ins = sum_squares(half, t)
            ins.then_inc(s_ssq, 1)
            ahead()
            x_hi_parts()
            ahead()

            def keep_unit(dst, scale):
                done.step()
                act.wait_ge(s_free, done.now())
                nc.scalar.activation(dst, bank[(done.n - SPLIT - 1) % 2][:, :], ACT.Copy,
                                     scale=scale).then_inc(s_qkv, c[s_qkv].step())

            def probabilities(n):
                act.wait_ge(s_max, n + 1)
                for qt, cols in enumerate((slice(0, P), slice(P, SEEN))):
                    ins = nc.scalar.activation(a_s[:, n % 2, :, cols], a_s[:, n % 2, :, cols], ACT.Exp,
                                               bias=nmax[:, n % 2, qt:qt + 1], accum_out=zsum[:, n % 2, qt:qt + 1])
                ins.then_inc(s_exp, 1)

            def keep_transposed(n):
                for g in range(G):
                    m = n * G + g
                    act.wait_ge(s_pT, m + 1)
                    if m >= 2:
                        act.wait_ge(s_pv, m - 1)
                    nc.scalar.activation(a_pT[:, m % 2], bank[5][:, 0:SEEN], ACT.Copy).then_inc(s_pTread, 1)

            for q in range(QUARTERS + 1):
                for u in range(DIL_UNITS):
                    if q < QUARTERS:
                        ahead()
                        g, part = divmod(u, 3)
                        if q >= 2 and u == 0:
                            act.wait_ge(s_pv, (q - 1) * QH * G)
                        keep_unit((a_qT, a_kT, a_v)[part][:, q % 2, g], DH ** -0.5 if part == 0 else 1.0)
                    if q == 0:
                        continue
                    n = (q - 1) * QH + u // 2
                    if u == 0:
                        probabilities(n)
                    elif u % 2 == 1:
                        keep_transposed(n)
                    elif u // 2 < QH:
                        probabilities(n)
                    if q == QUARTERS - 1 and u == 2:
                        y_hi_parts()
                        y_hi_parts()
                    if q == QUARTERS and u == 0:
                        y_hi_parts()
                    if q == QUARTERS and u in (2, 4):
                        ahead()
            y_hi_parts()
            ahead()
            ahead()
            done.step(OUT_SLABS)

            norm(1)
            x_hi_parts()

            def gate(j):
                done.step(2)
                act.wait_ge(s_free, done.now())
                if j >= 2:
                    act.wait_ge(s_gu, j - 1)
                nc.scalar.activation(f_sg[:, j % 2], bank[4 + 2 * (j % 2)][:, :], ACT.Silu).then_inc(s_silu, 1)
                act.wait_ge(s_gu, j + 1)
                nc.scalar.activation(f_hi[:, 2 * j:2 * j + 2].rearrange("p a t -> p (a t)"), f_h[:, j % 2],
                                     ACT.Copy).then_inc(s_fhi, 1)

            for j in range(GU_CHUNKS):
                ahead()
                ahead()
                gate(j)
            for _ in range(2 * DOWN_GROUPS):
                ahead()
            done.step(2 * DOWN_GROUPS)

            norm(2)
            x_hi_parts()

            nc.scalar.preload_act_table_set("natural_log_exp_and_others")
            step = Count(s_astep)

            def log_part(n):
                act.wait_ge(s_z, n + 1)
                if n >= 2:
                    act.wait_ge(s_sp, n - 1)
                nc.scalar.activation(b_l[:, n % 2], bank[2 + n % 2][:, 0:SEEN], ACT.Abs).then_inc(s_astep, step.step())
                act.wait_ge(s_astep, step.now())
                nc.scalar.activation(b_l[:, n % 2], b_l[:, n % 2], ACT.Exp, scale=-1.0).then_inc(s_astep, step.step())
                act.wait_ge(s_astep, step.now())
                nc.scalar.activation(b_l[:, n % 2], b_l[:, n % 2], ACT.Ln, bias=1.0).then_inc(s_astep, step.step())

            def head_slot(n):
                if n < H:
                    log_part(n)
                if 0 <= n - 1 < H:
                    m = n - 1
                    act.wait_ge(s_arg, m + 1)
                    if m >= 2:
                        act.wait_ge(s_o, m - 1)
                    nc.scalar.activation(b_att[:, m % 2], b_z[:, m % 2], ACT.Exp).then_inc(s_att, 1)
                if n - 2 >= 0 and n % 2 == 1:
                    m = n - 2
                    act.wait_ge(s_o, m + 1)
                    nc.scalar.activation(y_hi[:, m // 2], bank[6][:, 0:T], ACT.Copy).then_inc(s_ohi, 1)

            for q in range(QUARTERS):
                for u in range(SB_UNITS):
                    ahead()
                    middle, end = HEADS_IN.get(q * SB_UNITS + u, ([], []))
                    for n in middle:
                        head_slot(n)
                    dst = (b_qT[:, 2 * q:2 * q + 2].rearrange("p b t -> p (b t)"),
                           b_kT[:, 2 * q:2 * q + 2].rearrange("p b t -> p (b t)"), b_v[:, q])[u]
                    keep_unit(dst, DH ** -0.5 if u == 0 else 1.0)
                    for n in end:
                        head_slot(n)
            for n in range(12, H + 2):
                head_slot(n)
                if n in (12, 13):
                    ahead()
            ahead()
            ahead()
            done.step(OUT_SLABS)

            norm(3)
            act.wait_ge(s_wrt, 16)
            nc.scalar.activation(w_rt2[:, :, 0], w_rt[:, :, :], ACT.Copy).then_inc(s_rthi, 1)
            x_hi_parts()
            act.wait_ge(s_lgT, 1)
            nc.scalar.activation(lgT[:, :], bank[4][0:2 * NE, 0:T], ACT.Copy).then_inc(s_lgTread, 1)
            act.wait_ge(s_diff, 1)
            nc.scalar.activation(small["e"][:, :], small["d"][:, :], ACT.Exp).then_inc(s_e2, 1)
            nc.scalar.preload_act_table_set("silu_and_others")

            def tokens_hi():
                for b in range(2):
                    c[s_xg].step()
                    act.wait_ge(s_xg, c[s_xg].now())
                    nc.scalar.activation(
                        g_hi[:, 4 * b:4 * b + 4].rearrange("p k s -> p (k s)"), bank[6 + b][:, :],
                        ACT.Copy).then_inc(s_ghi, c[s_ghi].step())

            tokens_hi()
            act.wait_ge(s_routed, 1)
            turns = act.value_load(turns_i[0:1, 0:1], min_val=NE, max_val=2 * NE)
            with act.Fori(0, turns) as item:
                c.enter(ITEM, item)
                done.enter(item, FFN_SLABS)
                for f in filled:
                    f.enter(item, 16 * FFN_SLABS // RAW)

                def silu(j):
                    done.step(2)
                    act.wait_ge(s_free, done.now())
                    act.wait_ge(s_mread, c[s_mread].now(1 if j >= 2 else 0))
                    nc.scalar.activation(m_sg[:, j % 2], bank[j % 2][:, 0:256],
                    ACT.Silu).then_inc(s_msilu, c[s_msilu].step())
                    c[s_mread].step()

                def hidden_hi(j):
                    c[s_mT].step()
                    act.wait_ge(s_mT, c[s_mT].now())
                    nc.scalar.activation(m_hi[:, 2 * j:2 * j + 2].rearrange("p a s -> p (a s)"),
                                                         bank[2 + j % 2][:, 0:256],
                                                         ACT.Copy).then_inc(s_mhi, c[s_mhi].step())

                for j in range(GU_CHUNKS):
                    ahead()
                    ahead()
                    silu(j)
                    if j >= 1:
                        hidden_hi(j - 1)
                    if j == 4:
                        c[s_putT].step()
                        act.wait_ge(s_putT, c[s_putT].now())
                        nc.scalar.activation(slot_gate[:, :], bank[6][:, T:T + 1], ACT.Copy)
                        nc.scalar.activation(put[:, :], bank[6][:, 0:T], ACT.Copy).then_inc(s_put, c[s_put].step())
                def keep_y(half):
                    done.step()
                    act.wait_ge(s_free, done.now())
                    if half == 0:
                        act.wait_ge(s_put, c[s_put].now())
                    nc.scalar.activation(out_hi[:, half * SN:(half + 1) * SN], bank[4 + half][:, :], ACT.Copy,
                                         scale=slot_gate[:, 0:1]).then_inc(s_outhi, c[s_outhi].step())

                done.step(2 * DOWN_GROUPS - 2)
                for kg in range(DOWN_GROUPS):
                    ahead()
                    if kg == DOWN_GROUPS - 1:
                        keep_y(0)
                    ahead()
                    if kg == 0:
                        hidden_hi(GU_CHUNKS - 1)
                    if kg == 1:
                        tokens_hi()
                    if kg == DOWN_GROUPS - 1:
                        keep_y(1)
                c.leave(ITEM, turns, {s_hi, s_free, s_mread, s_msilu, s_mT, s_mhi, s_putT, s_put, s_xg,
                                      s_ghi, s_outhi})
                done.leave(turns)
                for f in filled:
                    f.leave(turns)
            for half in range(2):
                for t in range(TT):
                    c[s_added].step()
                    act.wait_ge(s_added, c[s_added].now())
                    ins = sum_squares(half, t)
            ins.then_inc(s_ssq, 1)

        @block.vector
        def _(dve):
            slabs, c = Slabs(), counts_of()
            done = Count(s_free, SPLIT)

            def lo():
                a, b = slabs.next()
                c[s_hi].step()
                dve.wait_ge(s_hi, c[s_hi].now())
                nc.vector.tensor_tensor(w_lo[:, b], raw[:, a], w_hi[:, b].bitcast(F32),
                                                          ALU.subtract).then_inc(s_split, c[s_split].step())

            n_norm = [0]
            steps = Count(s_nstep)

            def inverse_root():
                def link(ins):
                    ins.then_inc(s_nstep, steps.step())
                    dve.wait_ge(s_nstep, steps.now())

                link(nc.vector.scalar_tensor_tensor(out=total[:, :], in0=ssq[:, 0], scalar=D * EPS, in1=ssq[:, 1],
                                                    op0=ALU.add, op1=ALU.add))
                nc.vector.tensor_scalar(mean[:, :], total[:, :], -0.5 / D, None, ALU.mult)
                link(nc.vector.tensor_scalar(guess[:, :], total[:, :].bitcast(I32), 1, None, ALU.logical_shift_right))
                link(nc.vector.tensor_scalar(rstd[:, :].bitcast(I32), guess[:, :], -1.0,
                                             float(0x5F3759DF + (ROOT_D_BITS << 23)), ALU.mult, ALU.add))
                for _ in range(3):
                    for t in range(TT):
                        ins = nc.vector.scalar_tensor_tensor(
                            out=newton[:, t:t + 1], in0=rstd[:, t:t + 1], scalar=mean[:, t:t + 1],
                            in1=rstd[:, t:t + 1], op0=ALU.mult, op1=ALU.mult)
                    link(ins)
                    link(nc.vector.scalar_tensor_tensor(out=rstd[:, :], in0=newton[:, :], scalar=1.5, in1=rstd[:, :],
                                                        op0=ALU.add, op1=ALU.mult))

            def norm():
                n = n_norm[0]
                n_norm[0] += 1
                dve.wait_ge(s_ssq, n + 1)
                inverse_root()
                dve.wait_ge(s_gain, 16 * (n + 1))
                for half in range(2):
                    cols = slice(half * SN, (half + 1) * SN)
                    for t in range(TT):
                        nc.vector.scalar_tensor_tensor(out=hn[:, t, cols], in0=h[:, t, cols],
                                                       scalar=rstd[:, t:t + 1], in1=gains[:, cols],
                                                       op0=ALU.mult, op1=ALU.mult).then_inc(s_hn, 1)

            def x_lo_parts():
                for b in range(4):
                    k = slice(2 * b, 2 * b + 2)
                    c[s_xhi].step()
                    dve.wait_ge(s_xhi, c[s_xhi].now())
                    nc.vector.tensor_tensor(x_lo[:, k].rearrange("p k t -> p (k t)"), bank[b][:, :],
                                            x_hi[:, k].rearrange("p k t -> p (k t)").bitcast(F32),
                                            ALU.subtract).then_inc(s_xlo, 1)

            def add_chunk(ch, banks):
                done.step()
                cols = slice(ch * SN, (ch + 1) * SN)
                if ch == 1:
                    c[s_first].step()
                    dve.wait_ge(s_first, c[s_first].now())
                for t in range(TT):
                    if ch == 0 or t == 1:
                        dve.wait_ge(s_free, done.now())
                    nc.vector.tensor_tensor(h[:, t, cols], h[:, t, cols], bank[banks[t]][:, :],
                                            ALU.add).then_inc(s_h, 1)

            def ahead():
                lo()

            def y_lo_parts():
                c[s_xhi].step()
                b = (c[s_xhi].n - 1) % 4
                leading, trailing = (tile[:, 2 * b:2 * b + 2].rearrange("p k t -> p (k t)")
                                     for tile in ((d_hi, d_lo) if b < 2 else (x_hi, x_lo)))
                dve.wait_ge(s_xhi, c[s_xhi].now())
                nc.vector.tensor_tensor(trailing, bank[(4, 6, 4, 2)[b]][:, :], leading.bitcast(F32),
                                        ALU.subtract).then_inc(s_xlo, 1)

            nc.vector.sem_inc(s_split, RAW)
            norm()
            ahead()
            x_lo_parts()
            ahead()
            dve.wait_ge(s_const, 1)
            for g, stride in ((1, 4), (2, 16)):
                m = a_s[:, 0, g - 1].bitcast(I32)
                nc.vector.tensor_scalar(m, d_int[:, :], stride - 1, None, ALU.bitwise_and).then_inc(s_dint, 1)
                dve.wait_ge(s_dint, 3 * (g - 1) + 1)
                nc.vector.tensor_scalar(a_s[:, 1, g - 1], m, 0.0, MASKED, ALU.not_equal,
                                        ALU.mult).then_inc(s_dint, 1)
                dve.wait_ge(s_dint, 3 * (g - 1) + 2)
                nc.vector.tensor_tensor(dist[:, g], a_s[:, 1, g - 1], dist[:, 0],
                                        ALU.add).then_inc(s_dint, 1)
            dve.wait_ge(s_dmask, 2)

            def bias_scores(n):
                for g in range(G):
                    m = n * G + g
                    dve.wait_ge(s_scores, m + 1)
                    if n >= 2:
                        dve.wait_ge(s_pT, (n - 1) * G)
                    nc.vector.scalar_tensor_tensor(out=a_s[:, n % 2, g], in0=dist[:, g], scalar=negslope[:, n:n + 1],
                                                   in1=bank[2 + m % 2][:, 0:SEEN], op0=ALU.mult,
                                                   op1=ALU.add).then_inc(s_scread, 1)
                dve.wait_ge(s_scread, (n + 1) * G)
                for qt, cols in enumerate((slice(0, P), slice(P, SEEN))):
                    ins = nc.vector.tensor_reduce(nmax[:, n % 2, qt:qt + 1], a_s[:, n % 2, :, cols], AX.XY, ALU.max,
                                                  negate=True)
                ins.then_inc(s_max, 1)

            def finish_head(n):
                dve.wait_ge(s_pv, (n + 1) * G)
                nc.vector.reciprocal(zinv[:, :], zsum[:, n % 2]).then_inc(s_zinv, 1)
                dve.wait_ge(s_zinv, n + 1)
                nc.vector.tensor_tensor(hn[:, :, n * DH:(n + 1) * DH],
                                        bank[7][:, 0:TT * DH].rearrange("p (a d) -> p a d", a=TT),
                                        zinv[:, :].unsqueeze(2).to_broadcast([P, TT, DH]), ALU.mult).then_inc(s_y, 1)

            for q in range(QUARTERS + 1):
                for u in range(DIL_UNITS):
                    if q < QUARTERS:
                        ahead()
                    if q == 0:
                        continue
                    n = (q - 1) * QH + u // 2
                    if u == 0:
                        bias_scores(n)
                    elif u % 2 == 0:
                        finish_head(n - 1)
                    elif u // 2 < QH - 1:
                        bias_scores(n + 1)
                    if q == QUARTERS - 1 and u == 2:
                        y_lo_parts()
                        y_lo_parts()
                    if q == QUARTERS and u == 0:
                        y_lo_parts()
                    if q == QUARTERS and u in (2, 4):
                        ahead()
            y_lo_parts()
            ahead()
            done.step(QUARTERS * DIL_UNITS + OUT_SLABS - 2)
            add_chunk(0, (0, 1))
            add_chunk(1, (4, 6))

            norm()
            x_lo_parts()
            ahead()

            def gated(j):
                dve.wait_ge(s_silu, j + 1)
                if j >= 2:
                    dve.wait_ge(s_flo, j - 1)
                nc.vector.tensor_tensor(f_h[:, j % 2], f_sg[:, j % 2], bank[4 + 2 * (j % 2) + 1][:, :],
                                        ALU.mult).then_inc(s_gu, 1)

            for j in range(GU_CHUNKS):
                ahead()
                ahead()
                gated(j)
            for _ in range(2 * DOWN_GROUPS - 1):
                ahead()
            done.step(FFN_SLABS - 2)
            add_chunk(0, (0, 2))
            add_chunk(1, (1, 3))

            norm()
            x_lo_parts()
            ahead()
            dve.wait_ge(s_const, 7)

            def head_slot(n):
                if n < H:
                    dve.wait_ge(s_astep, 3 * (n + 1))
                    if n >= 2:
                        dve.wait_ge(s_cum, n - 1)
                    z = bank[2 + n % 2][:, 0:SEEN]
                    nc.vector.scalar_tensor_tensor(out=b_sp[:, n % 2], in0=z, scalar=0.0, in1=b_l[:, n % 2],
                                                   op0=ALU.max, op1=ALU.add).then_inc(s_sp, 1)
                    if n >= 2:
                        dve.wait_ge(s_att, n - 1)
                    nc.vector.tensor_tensor(b_z[:, n % 2], z, hide[:, :], ALU.add).then_inc(s_zread, 1)
                if 0 <= n - 1 < H:
                    m = n - 1
                    dve.wait_ge(s_zread, m + 1)
                    dve.wait_ge(s_cum, m + 1)
                    nc.vector.tensor_tensor(b_z[:, m % 2], b_z[:, m % 2], bank[4][:, 0:SEEN],
                                            ALU.subtract).then_inc(s_arg, 1)
                if n - 2 >= 0 and n % 2 == 1:
                    b = (n - 2) // 2
                    dve.wait_ge(s_ohi, b + 1)
                    nc.vector.tensor_tensor(y_lo[:, b], bank[6][:, 0:T], y_hi[:, b].bitcast(F32),
                                            ALU.subtract).then_inc(s_olo, 1)

            for q in range(QUARTERS):
                for u in range(SB_UNITS):
                    ahead()
                    middle, end = HEADS_IN.get(q * SB_UNITS + u, ([], []))
                    for n in middle + end:
                        head_slot(n)
            for n in range(12, H + 2):
                head_slot(n)
                if n in (12, 13):
                    ahead()
            ahead()
            done.step(QUARTERS * SB_UNITS + OUT_SLABS - 2)
            add_chunk(0, (0, 1))
            add_chunk(1, (5, 7))

            norm()
            dve.wait_ge(s_rthi, 1)
            nc.vector.tensor_tensor(w_rt2[:, :, 1], w_rt[:, :, :], w_rt2[:, :, 0].bitcast(F32),
                                    ALU.subtract).then_inc(s_rtlo, 1)
            x_lo_parts()
            ahead()
            route = Count(s_rstep)

            def link(ins):
                ins.then_inc(s_rstep, route.step())
                dve.wait_ge(s_rstep, route.now())

            def over_experts(v):
                return v[:, :].unsqueeze(2).to_broadcast([P, TT, NE])

            def first_of_max(lg, m, cand1, one):
                link(nc.vector.tensor_reduce(small[m][:, :], lg, AX.X, ALU.max))
                for t in range(TT):
                    ins = nc.vector.scalar_tensor_tensor(out=r["cand"][:, t], in0=lg[:, t],
                                                         scalar=small[m][:, t:t + 1], in1=r["rev"][:, t],
                                                         op0=ALU.is_equal, op1=ALU.mult)
                link(ins)
                link(nc.vector.tensor_reduce(small[cand1][:, :], r["cand"][:, :, :], AX.X, ALU.max))
                return nc.vector.tensor_tensor(r[one][:, :, :], r["rev"][:, :, :], over_experts(small[cand1]),
                                               ALU.is_equal)

            dve.wait_ge(s_clear, 1)
            dve.wait_ge(s_lg, 1)
            logits = bank[6][:, 0:TT * NE].rearrange("p (t e) -> p t e", t=TT)
            link(first_of_max(logits, "m1", "c1", "one1"))
            link(nc.vector.scalar_tensor_tensor(out=r["lg2"][:, :, :], in0=r["one1"][:, :, :], scalar=-3e38,
                                                in1=logits, op0=ALU.mult, op1=ALU.add))
            link(first_of_max(r["lg2"][:, :, :], "m2", "c2", "one2"))
            nc.vector.tensor_tensor(r["took"][:, :, :], r["one1"][:, :, :], r["one2"][:, :, :],
                                    ALU.add).then_inc(s_took, 1)
            nc.vector.tensor_tensor(small["d"][:, :], small["m2"][:, :], small["m1"][:, :],
                                    ALU.subtract).then_inc(s_diff, 1)
            dve.wait_ge(s_took, 1)
            dve.wait_ge(s_rank, 1)
            rank = bank[5][:, 0:TT * NE].rearrange("p (t e) -> p t e", t=TT)
            link(nc.vector.scalar_tensor_tensor(out=r["rank"][:, :, :], in0=rank, scalar=1.0, in1=r["took"][:, :, :],
                                                op0=ALU.add, op1=ALU.mult))
            nc.vector.tensor_scalar(slot_of[:, :, NE:2 * NE], r["rank"][:, :, :], -1.0 - P, None, ALU.add)
            link(nc.vector.tensor_scalar(slot_of[:, :, 0:NE], r["rank"][:, :, :], -1.0, None, ALU.add))

            def pick_tokens(item):
                dve.wait_ge(s_xg, c[s_xg].now())
                for t in range(TT):
                    ins = nc.vector.tensor_scalar(pick[:, t], slot_no[:, :], slot_of[:, t, bass.ds(item, 1)], None,
                                                  ALU.is_equal)
                ins.then_inc(s_pick, c[s_pick].step())

            def tokens_lo():
                for b in range(2):
                    k = slice(4 * b, 4 * b + 4)
                    c[s_ghi].step()
                    dve.wait_ge(s_ghi, c[s_ghi].now())
                    nc.vector.tensor_tensor(
                        g_lo[:, k].rearrange("p k s -> p (k s)"), bank[6 + b][:, :],
                        g_hi[:, k].rearrange("p k s -> p (k s)").bitcast(F32),
                        ALU.subtract).then_inc(s_glo, c[s_glo].step())

            def add_expert(half, banks):
                cols = slice(half * SN, (half + 1) * SN)
                for t in range(TT):
                    c[s_scat].step()
                    dve.wait_ge(s_scat, c[s_scat].now())
                    nc.vector.tensor_tensor(h[:, t, cols], h[:, t, cols], bank[banks[t]][:, :],
                                            ALU.add).then_inc(s_added, c[s_added].step())

            pick_tokens(0)
            c[s_xg].step(2)
            link(nc.vector.tensor_reduce(most[:, :], bank[5][:, TT * NE:TT * NE + NE], AX.X, ALU.max))
            link(nc.vector.tensor_scalar(turns_f[:, :], most[:, :], float(P), float(NE), ALU.is_gt, ALU.mult))
            nc.vector.tensor_scalar(turns_i[:, :], turns_f[:, :], float(NE), None, ALU.add).then_inc(s_routed, 1)
            tokens_lo()
            dve.wait_ge(s_e2, 1)
            link(nc.vector.tensor_scalar(small["den"][:, :], small["e"][:, :], 1.0, None, ALU.add))
            link(nc.vector.reciprocal(small["w1"][:, :], small["den"][:, :]))
            link(nc.vector.tensor_tensor(small["w2"][:, :], small["w1"][:, :], small["e"][:, :], ALU.mult))
            link(nc.vector.tensor_tensor(r["gate"][:, :, :], r["one1"][:, :, :], over_experts(small["w1"]), ALU.mult))
            link(nc.vector.tensor_tensor(r["tmp"][:, :, :], r["one2"][:, :, :], over_experts(small["w2"]), ALU.mult))
            for n in range(2):
                link(nc.vector.tensor_tensor(gate_of[:, :, n * NE:(n + 1) * NE], r["gate"][:, :, :], r["tmp"][:, :, :],
                                             ALU.add))
            dve.wait_ge(s_routed, 1)
            turns = dve.value_load(turns_i[0:1, 0:1], min_val=NE, max_val=2 * NE)

            with dve.Fori(0, turns) as item:
                c.enter(ITEM, item)

                def hidden(j):
                    c[s_msilu].step()
                    dve.wait_ge(s_msilu, c[s_msilu].now())
                    dve.wait_ge(s_mT, c[s_mT].now(1 if j >= 2 else 0))
                    nc.vector.tensor_tensor(m_h[:, j % 2], m_sg[:, j % 2], bank[j % 2][:, 256:512],
                                                              ALU.mult).then_inc(s_mread, c[s_mread].step())
                    c[s_mT].step()

                def hidden_lo(j):
                    k = slice(2 * j, 2 * j + 2)
                    c[s_mhi].step()
                    dve.wait_ge(s_mhi, c[s_mhi].now())
                    nc.vector.tensor_tensor(
                        m_lo[:, k].rearrange("p a s -> p (a s)"), bank[2 + j % 2][:, 0:256],
                        m_hi[:, k].rearrange("p a s -> p (a s)").bitcast(F32),
                        ALU.subtract).then_inc(s_mlo, c[s_mlo].step())

                for j in range(GU_CHUNKS):
                    ahead()
                    ahead()
                    hidden(j)
                    if j >= 1:
                        hidden_lo(j - 1)
                    if j == 1:
                        add_expert(0, (6, 7))
                    if j == 2:
                        add_expert(1, (6, 7))
                    if j == 3:
                        dve.wait_ge(s_putT, c[s_putT].now())
                        for t in range(TT):
                            ins = nc.vector.tensor_scalar(gate_now[:, t:t + 1], ones[:, 0:1],
                                                          gate_of[:, t, bass.ds(item, 1)], None, ALU.mult)
                        ins.then_inc(s_gate, c[s_gate].step())
                        c[s_putT].step()
                def keep_y(half):
                    cols = slice(half * SN, (half + 1) * SN)
                    c[s_outhi].step()
                    dve.wait_ge(s_outhi, c[s_outhi].now())
                    nc.vector.scalar_tensor_tensor(
                        out=out_lo[:, cols], in0=bank[4 + half][:, :], scalar=slot_gate[:, 0:1],
                        in1=out_hi[:, cols].bitcast(F32), op0=ALU.mult,
                        op1=ALU.subtract).then_inc(s_outlo[half], c[s_outlo[half]].step())

                for kg in range(DOWN_GROUPS):
                    ahead()
                    if kg == DOWN_GROUPS - 1:
                        keep_y(0)
                    ahead()
                    if kg == DOWN_GROUPS - 1:
                        keep_y(1)
                    if kg == 0:
                        hidden_lo(GU_CHUNKS - 1)
                    if kg == 0:
                        dve.wait_ge(s_putT, c[s_putT].now())
                        pick_tokens(item + 1)
                        c[s_xg].step(2)
                    if kg == 1:
                        tokens_lo()
                c.leave(ITEM, turns, {s_hi, s_split, s_pick, s_xg, s_ghi, s_glo, s_msilu, s_mT, s_mread, s_mhi, s_mlo,
                                      s_scat, s_added, s_putT, s_gate, s_outhi, *s_outlo})
            add_expert(0, (6, 7))
            add_expert(1, (0, 1))
            norm()

        @block.tensor
        def _(pe):
            slabs, c = Slabs(), counts_of()
            split = Count(s_split, RAW)

            def matmul(*a, **k):
                return nc.tensor.matmul(*a, **k)

            def next_slab():
                _, b = slabs.next()
                c[s_split].step()
                pe.wait_ge(s_split, c[s_split].now())
                return b

            def three(dst, left, right, start, stop):
                (lh, ll), (rh, rl) = left, right
                matmul(dst, lh, rh, start=start, stop=False)
                matmul(dst, ll, rh, start=False, stop=False)
                return matmul(dst, lh, rl, start=False, stop=stop)

            def wait_tile(k):
                if k % 2 == 0 and new_x[0]:
                    c[s_xlo].step()
                    pe.wait_ge(s_xlo, c[s_xlo].now())
                    new_x[0] -= 1

            new_x = [0]

            def unit(dst, features, between=None):
                b = next_slab()
                hi_, lo_ = (w[:, b].rearrange("p k (a n) -> p (k a) n", a=2) for w in (w_hi, w_lo))
                two = {"skip_group_check": True}
                for k in range(KT):
                    if k == KT // 2 and between:
                        between()
                    wait_tile(k)
                    for a in range(2):
                        out_ = dst[:, a * T:(a + 1) * T]
                        cols = slice(a * P, (a + 1) * P)
                        first, last = k == 0 and a == 0, k == KT - 1
                        if features:
                            (sh, sl), (mh, ml) = (hi_[:, k, cols], lo_[:, k, cols]), (x_hi[:, k], x_lo[:, k])
                        else:
                            (sh, sl), (mh, ml) = (x_hi[:, k, cols], x_lo[:, k, cols]), (hi_[:, k], lo_[:, k])
                        matmul(out_, sh, mh, start=first, stop=False, **two)
                        matmul(out_, sl, mh, start=False, stop=False, **two)
                        ins = matmul(out_, sh, ml, start=False, stop=last, **two)
                ins.then_inc(s_free, c[s_free].step())

            held = {}

            def out_part(ch, kh, part, banks, xh, xl, parts=2):
                if part == 0:
                    held[ch] = next_slab()
                b = held[ch]
                last = kh == 1 and part == parts - 1
                for t in range(TT):
                    tok = slice(t * P, (t + 1) * P)
                    for kl in range(part * SK // parts, (part + 1) * SK // parts):
                        k = kh * SK + kl
                        ins = three(bank[banks[ch][t]][:, :], (xh[:, k, tok], xl[:, k, tok]),
                                    (w_hi[:, b, kl], w_lo[:, b, kl]), start=k == 0, stop=k == KT - 1)
                    if last and ch == 1 and t == 0:
                        ins.then_inc(s_first, 1)
                if part == parts - 1:
                    ins.then_inc(s_free, c[s_free].step())

            def out_slab(ch, kh, banks, xh, xl):
                out_part(ch, kh, 0, banks, xh, xl, parts=1)

            def by_features(banks):
                for kh in range(2):
                    b = next_slab()
                    for kl in range(SK):
                        k = kh * SK + kl
                        wait_tile(k)
                        for blk in range(4):
                            f = slice(blk * P, (blk + 1) * P)
                            dst = banks[blk // 2][:, (blk % 2) * T:(blk % 2 + 1) * T]
                            first, last = k == 0 and blk % 2 == 0, k == KT - 1
                            two = {"skip_group_check": True}
                            matmul(dst, w_hi[:, b, kl, f], x_hi[:, k], start=first, stop=False, **two)
                            matmul(dst, w_hi[:, b, kl, f], x_lo[:, k], start=False, stop=False, **two)
                            ins = matmul(dst, w_lo[:, b, kl, f], x_hi[:, k], start=False, stop=last, **two)
                    ins.then_inc(s_free, c[s_free].step())

            def transpose_pair(b, dst, cols):
                for kk in range(2):
                    for t in range(TT):
                        ins = nc.tensor.transpose(dst[:, kk * T + t * P:kk * T + (t + 1) * P],
                                                  hn[:, t, cols(2 * b + kk)], ident[:, :])
                ins.then_inc(s_xT, c[s_xT].step())

            def transpose_x(cols):
                for half in range(2):
                    for t in range(TT):
                        c[s_hn].step()
                        pe.wait_ge(s_hn, c[s_hn].now())
                        for k in range(half * SK, (half + 1) * SK):
                            ins = nc.tensor.transpose(bank[k // 2][:, (k % 2) * T + t * P:(k % 2) * T + (t + 1) * P],
                                                      hn[:, t, cols(k)], ident[:, :])
                            if t == TT - 1 and k % 2 == 1:
                                ins.then_inc(s_xT, c[s_xT].step())
                new_x[0] = 4

            nc.tensor.sem_inc(s_free, SPLIT)
            pe.wait_ge(s_const, 2)
            transpose_x(plain_tile)

            tiles = ((slice(0, P), slice(0, P)), (slice(P, T), slice(0, P)), (slice(P, T), slice(P, T)))

            def qk_part(tile, n, g, tok):
                q, i = divmod(n, QH)
                rows = slice((i % 2) * DH, (i % 2 + 1) * DH)
                return tile[rows, q % 2, g, (i // 2) * T + tok.start:(i // 2) * T + tok.stop]

            def scores(n, g):
                m = n * G + g
                if m >= 2:
                    pe.wait_ge(s_scread, m - 1)
                s_ = bank[2 + m % 2]
                matmul(s_[:, 0:P], qk_part(a_qT, n, g, slice(0, P)), qk_part(a_kT, n, g, slice(0, P)),
                       start=True, stop=True)
                matmul(s_[:, P:SEEN], qk_part(a_qT, n, g, slice(P, T)), qk_part(a_kT, n, g, slice(0, T)),
                       start=True, stop=True).then_inc(s_scores, 1)

            def transpose_p(n, g):
                m = n * G + g
                if g == 0:
                    pe.wait_ge(s_exp, n + 1)
                if m >= 1:
                    pe.wait_ge(s_pTread, m)
                for a in range(3):
                    ins = nc.tensor.transpose(bank[5][:, a * P:(a + 1) * P],
                                              a_s[:, n % 2, g, a * P:(a + 1) * P], ident[:, :])
                ins.then_inc(s_pT, 1)

            def weigh_v(n, g):
                m, (q, i) = n * G + g, divmod(n, QH)
                pe.wait_ge(s_pTread, m + 1)
                if g == 0 and n >= 1:
                    pe.wait_ge(s_y, n)
                for a, (qt, kt) in enumerate(((0, 0), (1, 0), (1, 1))):
                    v = a_v[:, q % 2, g, kt * QN + i * DH:kt * QN + (i + 1) * DH]
                    ins = matmul(bank[7][:, qt * DH:(qt + 1) * DH], a_pT[:, m % 2, a * P:(a + 1) * P], v,
                                 start=g == 0 and a == 0, stop=g == G - 1 and a in (0, 2), skip_group_check=True)
                ins.then_inc(s_pv, 1)

            banks = ((0, 1), (4, 6))
            for q in range(QUARTERS + 1):
                for u in range(DIL_UNITS):
                    if q < QUARTERS:
                        if q * DIL_UNITS + u >= 2:
                            c[s_qkv].step()
                            pe.wait_ge(s_qkv, c[s_qkv].now())
                        unit(bank[(q * DIL_UNITS + u) % 2], u % 3 < 2)
                    if q == 0:
                        continue
                    n = (q - 1) * QH + u // 2
                    if u == 0:
                        pe.wait_ge(s_qkv, q * DIL_UNITS)
                        for g in range(G):
                            scores(n, g)
                        if q == QUARTERS:
                            pe.wait_ge(s_y, 3 * QH)
                            transpose_pair(2, bank[4], plain_tile)
                            pe.wait_ge(s_xlo, 6)
                            out_part(0, 0, 0, banks, d_hi, d_lo)
                    elif u % 2 == 1:
                        more = u // 2 < QH - 1
                        transpose_p(n, 0)
                        if more:
                            scores(n + 1, 0)
                        transpose_p(n, 1)
                        if more:
                            scores(n + 1, 1)
                        weigh_v(n, 0)
                        transpose_p(n, 2)
                        if more:
                            scores(n + 1, 2)
                        weigh_v(n, 1)
                    else:
                        if q == QUARTERS and u == 8:
                            out_part(0, 1, 1, banks, x_hi, x_lo, parts=4)
                        weigh_v(n - 1, 2)
                        if q == QUARTERS - 1 and u == 2:
                            pe.wait_ge(s_y, 2 * QH)
                            transpose_pair(0, bank[4], plain_tile)
                            transpose_pair(1, bank[6], plain_tile)
                        if q < QUARTERS:
                            continue
                        if u == 2:
                            out_part(0, 0, 1, banks, d_hi, d_lo)
                        if u == 4:
                            pe.wait_ge(s_xlo, 7)
                            out_part(1, 0, 0, banks, d_hi, d_lo)
                        if u == 6:
                            out_part(1, 0, 1, banks, d_hi, d_lo)
                            out_part(0, 1, 0, banks, x_hi, x_lo, parts=4)
            out_part(1, 1, 0, banks, x_hi, x_lo, parts=4)
            pe.wait_ge(s_y, H)
            transpose_pair(3, bank[2], plain_tile)
            out_part(1, 1, 1, banks, x_hi, x_lo, parts=4)
            c[s_xlo].step(4)
            pe.wait_ge(s_xlo, c[s_xlo].now())
            for ch in range(2):
                out_part(ch, 1, 1, banks, x_hi, x_lo)

            pe.wait_ge(s_h, 4)
            transpose_x(adjacent_tile)
            for j in range(GU_CHUNKS):
                if j >= 2:
                    pe.wait_ge(s_gu, j - 1)
                by_features([bank[4 + 2 * (j % 2) + n] for n in range(2)])
            pe.wait_ge(s_gu, GU_CHUNKS)
            for kg in range(DOWN_GROUPS):
                pe.wait_ge(s_flo, 2 * kg + 2)
                for half in range(2):
                    b = next_slab()
                    for t in range(TT):
                        tok = slice(t * P, (t + 1) * P)
                        for kl in range(SK):
                            k = kg * SK + kl
                            ins = three(bank[2 * t + half][:, :], (f_hi[:, k, tok], f_lo[:, k, tok]),
                                        (w_hi[:, b, kl], w_lo[:, b, kl]), start=k == 0, stop=k == FF // P - 1)
                        if kg == DOWN_GROUPS - 1 and half == 1 and t == 0:
                            ins.then_inc(s_first, 1)
                    ins.then_inc(s_free, c[s_free].step())

            pe.wait_ge(s_h, 8)
            transpose_x(plain_tile)

            def head_part(tile, n, tok):
                return tile[(n % 2) * DH:(n % 2 + 1) * DH, n // 2, tok]

            def head_slot(n):
                if n < H:
                    if n >= 2:
                        pe.wait_ge(s_zread, n - 1)
                    z = bank[2 + n % 2]
                    matmul(z[:, 0:T], head_part(b_kT, n, slice(0, P)), head_part(b_qT, n, slice(0, T)), start=True,
                           stop=True)
                    matmul(z[:, T:SEEN], head_part(b_kT, n, slice(P, T)), head_part(b_qT, n, slice(P, T)), start=True,
                           stop=True).then_inc(s_z, 1)
                if 0 <= n - 1 < H:
                    m = n - 1
                    pe.wait_ge(s_spm, m + 1)
                    if m >= 1:
                        pe.wait_ge(s_arg, m)
                    sums = bank[4]
                    matmul(sums[:, 0:SEEN], from_on[:, :], b_sp[:, m % 2], start=True, stop=False)
                    matmul(sums[:, P:T], ones[:, :], b_sp[:, m % 2, T:SEEN], start=False, stop=True).then_inc(s_cum, 1)
                if n - 2 >= 0:
                    m = n - 2
                    pe.wait_ge(s_att, m + 1)
                    if m >= 2 and m % 2 == 0:
                        pe.wait_ge(s_olo, m // 2)
                    q, i = divmod(m, QH)
                    rows = slice((m % 2) * DH, (m % 2 + 1) * DH)
                    o = bank[6]
                    for kt in range(2):
                        v = b_v[:, q, kt * QN + i * DH:kt * QN + (i + 1) * DH]
                        ins = matmul(o[rows, kt * P:T], v, b_att[:, m % 2, kt * T:T + kt * P], start=kt == 0,
                                     stop=kt == 1)
                    ins.then_inc(s_o, 1)

            read = QUARTERS * DIL_UNITS
            for q in range(QUARTERS):
                for u in range(SB_UNITS):
                    m = q * SB_UNITS + u
                    if m >= 2:
                        pe.wait_ge(s_qkv, read + m - 1)
                    middle, end = HEADS_IN.get(m, ([], []))

                    def heads_between():
                        if u == 0 and q > 0:
                            pe.wait_ge(s_qkv, read + q * SB_UNITS)
                        for n in middle:
                            head_slot(n)

                    unit(bank[m % 2], u < 2, heads_between)
                    for n in end:
                        head_slot(n)
            pe.wait_ge(s_qkv, read + QUARTERS * SB_UNITS)
            banks = ((0, 1), (5, 7))
            for n in range(12, H + 2):
                head_slot(n)
                if n in (12, 13):
                    pe.wait_ge(s_olo, 4)
                    out_slab(n - 12, 0, banks, y_hi, y_lo)
                if n in (14, 15):
                    pe.wait_ge(s_olo, 6)
                    out_part(n - 14, 1, 0, banks, y_hi, y_lo)
                if n == 16:
                    pe.wait_ge(s_olo, 7)
                    out_part(0, 1, 2, banks, y_hi, y_lo, parts=4)
            pe.wait_ge(s_olo, H // 2)
            out_part(0, 1, 3, banks, y_hi, y_lo, parts=4)
            out_part(1, 1, 1, banks, y_hi, y_lo)

            pe.wait_ge(s_h, 12)
            transpose_x(adjacent_tile)
            pe.wait_ge(s_rtlo, 1)
            for k in range(KT):
                wait_tile(k)
                for part, xx in enumerate((x_hi, x_lo)):
                    ins = matmul(bank[4][0:2 * NE, 0:T], w_rt2[:, k].rearrange("p a e -> p (a e)"), xx[:, k],
                                 start=k == 0 and part == 0, stop=k == KT - 1 and part == 1)
            ins.then_inc(s_lgT, 1)
            pe.wait_ge(s_clear, 1)
            pe.wait_ge(s_lgTread, 1)
            for t in range(TT):
                ins = matmul(bank[6][:, t * NE:(t + 1) * NE], lgT[:, t * P:(t + 1) * P], fold[:, :], start=True,
                             stop=True)
            ins.then_inc(s_lg, 1)
            pe.wait_ge(s_took, 1)
            took = r["took"]
            matmul(bank[5][:, 0:NE], before[:, :], took[:, 0], start=True, stop=True)
            matmul(bank[5][:, NE:2 * NE], ones[:, :], took[:, 0], start=True, stop=False)
            matmul(bank[5][:, NE:2 * NE], before[:, :], took[:, 1], start=False, stop=True)
            matmul(bank[5][:, 2 * NE:3 * NE], ones[:, :], took[:, 0], start=True, stop=False)
            matmul(bank[5][:, 2 * NE:3 * NE], ones[:, :], took[:, 1], start=False, stop=True).then_inc(s_rank, 1)

            def gather():
                c[s_pick].step()
                pe.wait_ge(s_pick, c[s_pick].now())
                for b in range(2):
                    for kk in range(4):
                        k = 4 * b + kk
                        for t in range(TT):
                            ins = matmul(bank[6 + b][:, kk * P:(kk + 1) * P], hn[:, t, adjacent_tile(k)], pick[:, t],
                                         start=t == 0, stop=t == TT - 1)
                    ins.then_inc(s_xg, c[s_xg].step())

            def scatter(half, banks):
                pe.wait_ge(s_outlo[half], c[s_outlo[half]].now())
                for t in range(TT):
                    if banks[t] >= 6:
                        pe.wait_ge(s_added, c[s_added].now())
                    matmul(bank[banks[t]][:, :], put[:, t * P:(t + 1) * P], out_hi[:, half * SN:(half + 1) * SN],
                           start=True, stop=False)
                    matmul(bank[banks[t]][:, :], put[:, t * P:(t + 1) * P], out_lo[:, half * SN:(half + 1) * SN],
                           start=False, stop=True).then_inc(s_scat, c[s_scat].step())
                c[s_added].step(2)

            gather()
            pe.wait_ge(s_routed, 1)
            turns = pe.value_load(turns_i[0:1, 0:1], min_val=NE, max_val=2 * NE)
            with pe.Fori(0, turns) as item:
                c.enter(ITEM, item)

                def transpose_hidden(j):
                    c[s_mread].step()
                    pe.wait_ge(s_mread, c[s_mread].now())
                    pe.wait_ge(s_mlo, c[s_mlo].now(1 if j >= 2 else 0))
                    for a in range(2):
                        ins = nc.tensor.transpose(bank[2 + j % 2][:, a * P:(a + 1) * P],
                                                  m_h[:, j % 2, a * P:(a + 1) * P], ident[:, :])
                    ins.then_inc(s_mT, c[s_mT].step())
                    c[s_mlo].step()

                c[s_glo].step(2)
                pe.wait_ge(s_glo, c[s_glo].now())
                for j in range(GU_CHUNKS):
                    for kh in range(2):
                        b = next_slab()
                        for kl in range(SK):
                            k = kh * SK + kl
                            ins = three(bank[j % 2][:, :], (g_hi[:, k], g_lo[:, k]), (w_hi[:, b, kl], w_lo[:, b, kl]),
                                        start=k == 0, stop=k == KT - 1)
                        ins.then_inc(s_free, c[s_free].step())
                    if j >= 1:
                        transpose_hidden(j - 1)
                    if j == 1:
                        scatter(0, (6, 7))
                    if j == 2:
                        scatter(1, (6, 7))
                    if j == 4:
                        c[s_gate].step()
                        pe.wait_ge(s_gate, c[s_gate].now())
                        pe.wait_ge(s_added, c[s_added].now())
                        for t in range(TT):
                            nc.tensor.transpose(bank[6][:, t * P:(t + 1) * P], pick[:, t], ident[:, :])
                        for t in range(TT):
                            ins = matmul(bank[6][:, T:T + 1], pick[:, t], gate_now[:, t:t + 1], start=t == 0,
                                         stop=t == TT - 1)
                        ins.then_inc(s_putT, c[s_putT].step())
                for kg in range(DOWN_GROUPS):
                    if kg == 1:
                        transpose_hidden(GU_CHUNKS - 1)
                    if kg == 0:
                        pe.wait_ge(s_mlo, c[s_mlo].now(GU_CHUNKS - 3))
                        pe.wait_ge(s_outlo[1], c[s_outlo[1]].now())
                    else:
                        pe.wait_ge(s_mlo, c[s_mlo].now(GU_CHUNKS - 2 * kg - 2))
                    for half in range(2):
                        b = next_slab()
                        for kl in range(SK):
                            k = kg * SK + kl
                            ins = three(bank[4 + half][:, :], (m_hi[:, k], m_lo[:, k]),
                                        (w_hi[:, b, kl], w_lo[:, b, kl]), start=k == 0, stop=k == FF // P - 1)
                        ins.then_inc(s_free, c[s_free].step())
                    if kg == 1:
                        c[s_put].step()
                        pe.wait_ge(s_put, c[s_put].now())
                        gather()
                for y in s_outlo:
                    c[y].step()
                c.leave(ITEM, turns, {s_split, s_free, s_glo, s_mread, s_mlo, s_mT, s_scat, s_added, s_gate,
                                      s_putT, s_put, s_pick, s_xg, *s_outlo})
            scatter(0, (6, 7))
            scatter(1, (0, 1))


_INS = ["x", "mix_norm", "ffn_norm", "dil_w_in", "dil_w_out", "sb_w_qkv", "sb_w_out", "ffn_w_gate_up", "ffn_w_down",
        "moe_w_router", "moe_w_gate_up", "moe_w_down", "final_norm"]


def kernel(**inputs):
    import concourse.bacc as bacc
    from concourse.bass_utils import run_bass_kernel_spmd

    nc = bacc.Bacc("TRN2", target_bir_lowering=False, num_devices=1)
    arrays, args = {}, []
    for name in _INS:
        a = np.ascontiguousarray(inputs[name])
        arrays[f"in_{name}"] = a
        args.append(nc.dram_tensor(f"in_{name}", a.shape, mybir.dt.from_np(a.dtype), kind="ExternalInput").ap())
    out = nc.dram_tensor("out", (1, T, D), F32, kind="ExternalOutput").ap()
    trunk(nc, *args, out)
    res = run_bass_kernel_spmd(nc, [arrays], core_ids=[0])
    return res.results[0]["out"]
```
